# Optimizing a Trainium2 kernel written in Bass

```python
import jax, jax.numpy as jnp
from jax import lax
import numpy as np

D_MODEL = 1024
BATCH = 1
SEQ = 2048
DEPTH = 1

HEAD_DIM = D_MODEL // 16
N_ATTN_HEADS = 8
N_KV_HEADS = 2
GQA_GROUP = N_ATTN_HEADS // N_KV_HEADS
WINDOW = 128
BLOCK = 128
N_CONV_GROUPS = 4
CONV_WIDTH = N_CONV_GROUPS * HEAD_DIM
CONV_K = 3
N_MEM_HEADS = 4
N_MEM = 256
ATTN_WIDTH = N_ATTN_HEADS * HEAD_DIM
KV_WIDTH = N_KV_HEADS * HEAD_DIM
MEM_WIDTH = N_MEM_HEADS * HEAD_DIM
MIX_WIDTH = ATTN_WIDTH + CONV_WIDTH + MEM_WIDTH
IN_PROJ_WIDTH = ATTN_WIDTH + 2 * KV_WIDTH + 3 * CONV_WIDTH + MEM_WIDTH
SPLIT_POINTS = (
    ATTN_WIDTH,
    ATTN_WIDTH + KV_WIDTH,
    ATTN_WIDTH + 2 * KV_WIDTH,
    ATTN_WIDTH + 2 * KV_WIDTH + CONV_WIDTH,
    ATTN_WIDTH + 2 * KV_WIDTH + 2 * CONV_WIDTH,
    ATTN_WIDTH + 2 * KV_WIDTH + 3 * CONV_WIDTH,
)
D_FF = ((8 * D_MODEL // 3 + 255) // 256) * 256
EPS = 1e-6
NEG_INF = -1e30

kernel_name = "hymba_conv_swa_memory_hybrid"

def rms_norm(x, g):
    xf = x.astype(jnp.float32)
    y = xf * lax.rsqrt(jnp.mean(xf * xf, axis=-1, keepdims=True) + EPS)
    return (y * g.astype(jnp.float32)).astype(x.dtype)

def alibi_slopes():
    return jnp.asarray(2.0 ** (-8.0 * np.arange(1, N_ATTN_HEADS + 1) / N_ATTN_HEADS), dtype=jnp.float32)

def sliding_window_attention(q, k, v, sinks):
    B, S = q.shape[0], q.shape[1]
    nb = S // BLOCK
    qb = q.reshape(B, nb, BLOCK, N_KV_HEADS, GQA_GROUP, HEAD_DIM)

    def band(t):
        tb = t.reshape(B, nb, BLOCK, N_KV_HEADS, HEAD_DIM)
        prev = jnp.pad(tb[:, :-1], ((0, 0), (1, 0), (0, 0), (0, 0), (0, 0)))
        return jnp.concatenate([prev, tb], axis=2)

    kb, vb = band(k), band(v)
    scores = jnp.einsum('bnqhgd,bnkhd->bnhgqk', qb, kb).astype(jnp.float32) * (HEAD_DIM ** -0.5)
    q_idx = jnp.arange(BLOCK)[:, None]
    k_idx = jnp.arange(2 * BLOCK)[None, :]
    dist = q_idx + BLOCK - k_idx
    key_pos = jnp.arange(nb)[:, None] * BLOCK - BLOCK + jnp.arange(2 * BLOCK)[None, :]
    valid = ((dist >= 0) & (dist < WINDOW))[None] & (key_pos >= 0)[:, None, :]
    slopes = alibi_slopes().reshape(N_KV_HEADS, GQA_GROUP)
    bias = -slopes[:, :, None, None] * dist.astype(jnp.float32)
    scores = jnp.where(valid[None, :, None, None], scores + bias[None, None], NEG_INF)
    sink = jnp.broadcast_to(sinks.astype(jnp.float32).reshape(1, 1, N_KV_HEADS, GQA_GROUP, 1, 1),
                            scores.shape[:-1] + (1,))
    probs = jax.nn.softmax(jnp.concatenate([scores, sink], axis=-1), axis=-1)[..., :-1]
    out = jnp.einsum('bnhgqk,bnkhd->bnqhgd', probs.astype(v.dtype), vb)
    return out.reshape(B, S, ATTN_WIDTH)

def short_gated_conv(h, b_gate, c_gate, conv_w, conv_b):
    S = h.shape[1]
    u = c_gate * h
    u_pad = jnp.pad(u, ((0, 0), (CONV_K - 1, 0), (0, 0)))
    conv = sum(conv_w[j] * u_pad[:, j:j + S] for j in range(CONV_K)) + conv_b
    return b_gate * conv

def memory_cross_attention(q, mem_n, w_mem_kv, mem_q_norm, mem_k_norm):
    B, S = q.shape[0], q.shape[1]
    q = rms_norm(q.reshape(B, S, N_MEM_HEADS, HEAD_DIM), mem_q_norm)
    kv = mem_n @ w_mem_kv
    k, v = jnp.split(kv, 2, axis=-1)
    k = rms_norm(k.reshape(B, -1, N_MEM_HEADS, HEAD_DIM), mem_k_norm)
    v = v.reshape(B, -1, N_MEM_HEADS, HEAD_DIM)
    scores = jnp.einsum('bshd,bmhd->bhsm', q, k).astype(jnp.float32) * (HEAD_DIM ** -0.5)
    probs = jax.nn.softmax(scores, axis=-1)
    out = jnp.einsum('bhsm,bmhd->bshd', probs.astype(v.dtype), v)
    return out.reshape(B, S, MEM_WIDTH)

def hybrid_mixer(xn, mem_n, w_in, q_norm, k_norm, attn_sinks, conv_w, conv_b, w_mem_kv,
                 mem_q_norm, mem_k_norm, out_norm_attn, out_norm_conv, out_norm_mem, w_out):
    B, S = xn.shape[0], xn.shape[1]
    proj = xn @ w_in
    q_a, k_a, v_a, c_h, c_b, c_c, q_m = jnp.split(proj, SPLIT_POINTS, axis=-1)
    q_a = rms_norm(q_a.reshape(B, S, N_ATTN_HEADS, HEAD_DIM), q_norm)
    k_a = rms_norm(k_a.reshape(B, S, N_KV_HEADS, HEAD_DIM), k_norm)
    v_a = v_a.reshape(B, S, N_KV_HEADS, HEAD_DIM)
    attn_out = sliding_window_attention(q_a, k_a, v_a, attn_sinks)
    conv_out = short_gated_conv(c_h, c_b, c_c, conv_w, conv_b)
    mem_out = memory_cross_attention(q_m, mem_n, w_mem_kv, mem_q_norm, mem_k_norm)
    merged = jnp.concatenate([rms_norm(attn_out, out_norm_attn),
                              rms_norm(conv_out, out_norm_conv),
                              rms_norm(mem_out, out_norm_mem)], axis=-1)
    return merged @ w_out

def swiglu_ffn(xn, w_gate, w_up, w_down):
    return (jax.nn.silu(xn @ w_gate) * (xn @ w_up)) @ w_down

def setup_inputs(seed: int = 0) -> dict:
    key = jax.random.key(seed)
    ks = jax.random.split(key, 24)
    f32 = jnp.float32

    def normal(k, shape, scale):
        return jax.random.normal(k, shape, f32) * scale

    def gain(k, shape):
        return 1.0 + 0.05 * jax.random.normal(k, shape, f32)

    L = DEPTH
    return {
        "x": jax.random.normal(ks[0], (BATCH, SEQ, D_MODEL), f32),
        "mem": jax.random.normal(ks[1], (BATCH, N_MEM, D_MODEL), f32),
        "norm_mix": gain(ks[2], (L, D_MODEL)),
        "w_in": normal(ks[3], (L, D_MODEL, IN_PROJ_WIDTH), D_MODEL ** -0.5),
        "q_norm": gain(ks[4], (L, HEAD_DIM)),
        "k_norm": gain(ks[5], (L, HEAD_DIM)),
        "attn_sinks": normal(ks[6], (L, N_ATTN_HEADS), 0.5),
        "conv_w": normal(ks[7], (L, CONV_K, CONV_WIDTH), CONV_K ** -0.5),
        "conv_b": normal(ks[8], (L, CONV_WIDTH), 0.01),
        "norm_mem": gain(ks[9], (L, D_MODEL)),
        "w_mem_kv": normal(ks[10], (L, D_MODEL, 2 * MEM_WIDTH), D_MODEL ** -0.5),
        "mem_q_norm": gain(ks[11], (L, HEAD_DIM)),
        "mem_k_norm": gain(ks[12], (L, HEAD_DIM)),
        "out_norm_attn": gain(ks[13], (L, ATTN_WIDTH)),
        "out_norm_conv": gain(ks[14], (L, CONV_WIDTH)),
        "out_norm_mem": gain(ks[15], (L, MEM_WIDTH)),
        "w_out": normal(ks[16], (L, MIX_WIDTH, D_MODEL), MIX_WIDTH ** -0.5),
        "norm_ffn": gain(ks[17], (L, D_MODEL)),
        "w_gate": normal(ks[18], (L, D_MODEL, D_FF), D_MODEL ** -0.5),
        "w_up": normal(ks[19], (L, D_MODEL, D_FF), D_MODEL ** -0.5),
        "w_down": normal(ks[20], (L, D_FF, D_MODEL), D_FF ** -0.5),
    }

def reference(x, mem, norm_mix, w_in, q_norm, k_norm, attn_sinks, conv_w, conv_b, norm_mem,
              w_mem_kv, mem_q_norm, mem_k_norm, out_norm_attn, out_norm_conv, out_norm_mem,
              w_out, norm_ffn, w_gate, w_up, w_down):
    for l in range(DEPTH):
        xn = rms_norm(x, norm_mix[l])
        mem_n = rms_norm(mem, norm_mem[l])
        x = x + hybrid_mixer(xn, mem_n, w_in[l], q_norm[l], k_norm[l], attn_sinks[l], conv_w[l],
                             conv_b[l], w_mem_kv[l], mem_q_norm[l], mem_k_norm[l],
                             out_norm_attn[l], out_norm_conv[l], out_norm_mem[l], w_out[l])
        x = x + swiglu_ffn(rms_norm(x, norm_ffn[l]), w_gate[l], w_up[l], w_down[l])
    return x


_drawn_inputs = setup_inputs


def setup_inputs(seed=0):
    import zlib

    import numpy as np

    out = dict(_drawn_inputs(seed))
    spreads = {}
    factors = {'q_norm': 7.289,
     'conv_b': 8.0,
     'mem_q_norm': 2.907,
     'mem_k_norm': 3.21,
     'out_norm_conv': 3.128,
     'out_norm_mem': 3.131,
     'attn_sinks': 6.304,
     'out_norm_attn': 3.966,
     'norm_ffn': 3.467}
    for name, (base, spread) in spreads.items():
        noise = np.random.default_rng([zlib.crc32(name.encode()), seed]).standard_normal(out[name].shape)
        drawn = base * np.exp(spread * noise) if base else spread * noise
        out[name] = __import__('jax').numpy.asarray(drawn.astype(out[name].dtype))
    for name, factor in factors.items():
        out[name] = (out[name] * factor).astype(out[name].dtype)
    return out
```

```python
from contextlib import ExitStack

import numpy as np

import concourse.bass as bass
from concourse import mybir

F32 = mybir.dt.float32
F32R = mybir.dt.float32r
ALU = mybir.AluOpType
ACT = mybir.ActivationFunctionType
AX_X = mybir.AxisListType.X

P = 128
D = 1024
DC = D // P
SEQ = 2048
TILES = SEQ // P
HD = 64
HEADS = 8
CONV_CH = 256
CC = CONV_CH // P
MEM = 256
MEM_HEADS = 4
MEM_W = MEM_HEADS * HD
UNITS = 6
SLOTS = 2 * UNITS
KEYS = 2 * P
QK = 512 + P + MEM_W
QK_HEADS = QK // HD
PROJ = 2 * QK
GROUP = 448
GROUPS = PROJ // GROUP
FF = 2816
PAIRS = FF // (2 * P)
HALF = SEQ // 2
HT = HALF // P
BANK = 512
EPS = 1e-6
MASKED = -1e30
ACT_SET = "natural_log_exp_and_others"

V0, H0, C0, B0 = 0, P, P + CONV_CH, P + 2 * CONV_CH
QG, KG, MQG, MKG, CW, CB, SINK, MEANS, EPS4, THREE, ONE, COLS = 0, 1, 2, 3, 4, 10, 12, 20, 23, 24, 25, 26
GROUP_CHUNKS = (range(0, 4), range(4, 6), range(6, 8))


def unit_heads(u):
    return 4 * (u % 2) + 2 * (u // 2) if u < 4 else 8 + 2 * (u - 4)


def unit_rows(u):
    e = u % 2
    return slice(HD * e, HD * e + HD)


class Steps:

    def __init__(self, engine, semaphore, per):
        self.engine, self.semaphore, self.per, self.round, self.k = engine, semaphore, per, 0, 0

    def start(self, i):
        self.round, self.k = i, 0

    def then_wait(self, instruction):
        self.k += 1
        assert self.k <= self.per
        instruction.then_inc(self.semaphore, 1)
        self.engine.wait_ge(self.semaphore, self.round * self.per + self.k)


def three_passes(pe, out, wh, wl, xh, xl, start, stop):
    pe.matmul(out, wh, xh, start=start, stop=False)
    pe.matmul(out, wh, xl, start=False, stop=False)
    return pe.matmul(out, wl, xh, start=False, stop=stop)


def rsqrt_table(act, steps, z, ln, v4):
    steps.then_wait(act.activation(ln, v4, ACT.Ln))
    return act.activation(z, ln, ACT.Exp, scale=-0.5)


def rsqrt_newton(pool, steps, z, v4, t, three):
    steps.then_wait(pool.tensor_tensor(t, z, z, ALU.mult))
    steps.then_wait(pool.tensor_tensor(t, t, v4, ALU.mult))
    steps.then_wait(pool.tensor_tensor(t, three, t, ALU.subtract))
    return pool.tensor_tensor(z, z, t, ALU.mult)


def mixer_phase(nc, x, mem, cols, gain_mix, gain_mem, masks, ident_d, w_in, w_mem, mixed, stats):
    with ExitStack() as ctx:
        def sb(name, shape, dt=F32):
            return ctx.enter_context(nc.sbuf_tensor(name, shape, dt))

        def sem(name):
            return ctx.enter_context(nc.semaphore(name))

        wh = sb("w_in_high", [P, DC, PROJ], F32R)
        wl = sb("w_in_low", [P, DC, PROJ], F32R)
        small = sb("small", [P, COLS])
        q8 = sb("q_gains_scaled", [P, 2])
        neg_sink = sb("neg_sink", [P, HEADS])
        gain = sb("gain_row", [P, D])
        mask = sb("mask", [P, HEADS, KEYS])
        ident = sb("ident", [P, P])
        xt = sb("xt", [P, D])
        xs = sb("xs", [P, D])
        with nc.sbuf_tensor("early_tiles", [P, 2, D], F32) as early_tiles:
            pass
        xh = sb("x_high", [P, DC, P], F32R)
        xl = sb("x_low", [P, DC, P], F32R)
        pq = sb("proj_qk", [P, QK])
        pv = sb("proj_vhcb", [P, QK])
        v2 = sb("v_prev_cur", [P, 2, P])
        qT = sb("qT", [P, 4, P])
        mqT = sb("mem_qT", [P, 2, P])
        kT = sb("kT_prev_cur", [P, KEYS])
        uT = sb("uT", [P, CC, P + 2])
        bT = sb("bT", [P, CC, P])
        cy = sb("conv_sum", [P, CC, P])
        scores = sb("scores", [P, HEADS, KEYS + 1])
        region = sb("region", [P, SLOTS * (KEYS + 1) + 2 * HEADS * P])
        probs = region[:, 0:SLOTS * (KEYS + 1)].rearrange("p (h k) -> p h k", k=KEYS + 1)
        pT = region[:, SLOTS * (KEYS + 1):].rearrange("p (b h q) -> p b h q", b=2, h=HEADS)
        w_mem_sb = region[:, 0:DC * 2 * MEM_W].rearrange("p (c n) -> p c n", c=DC)
        memT = region[:, DC * 2 * MEM_W:DC * 2 * MEM_W + D].rearrange("p (c n) -> p c n", c=DC)
        region2 = sb("region2", [P, 2 * D + PROJ])
        mpT = region2[:, 0:D].rearrange("p (b h q) -> p b h q", b=2, h=MEM_HEADS)
        mix = region2[:, D:2 * D].rearrange("p (c q) -> p c q", c=DC)
        squares = region2[:, 2 * D:3 * D]
        sqmix = squares.rearrange("p (c q) -> p c q", c=DC)
        stage = [region2[:, 0:PROJ], region2[:, 2 * D:2 * D + PROJ],
                 scores[:, :, :].rearrange("p h k -> p (h k)")[:, 0:PROJ],
                 mask[:, :, :].rearrange("p h k -> p (h k)")[:, 0:PROJ]]
        early = [xt[:, :], early_tiles[:, 0, :], early_tiles[:, 1, :]]
        km = [pq[:, 0:MEM_W], pv[:, 0:MEM_W]]
        km_sq = sb("mem_k_squares", [P, MEM_W])
        kmT = sb("mem_kT", [P, 2, MEM])
        vm = sb("mem_v", [P, 2, MEM_W])
        ssq = sb("ssq", [P, 1])
        xv = sb("x_var", [P, 1])
        xln = sb("x_ln", [P, 1])
        xr = sb("x_rstd", [P, 1])
        xn2 = sb("x_newton", [P, 1])
        qss = sb("qk_ss", [P, QK_HEADS])
        qv = sb("qk_var", [P, QK_HEADS])
        qln = sb("qk_ln", [P, QK_HEADS])
        qr = sb("qk_rstd", [P, QK_HEADS])
        qn2 = sb("qk_newton", [P, QK_HEADS])
        mx = sb("row_max", [P, SLOTS])
        nm = sb("neg_max", [P, SLOTS])
        rs = sb("row_sum", [P, SLOTS])
        rr = sb("row_rcp", [P, SLOTS])

        def bank(name):
            return ctx.enter_context(nc.psum_tensor(name, [P, BANK], F32))

        turn = [bank("turn0"), bank("turn1")]
        proj = [bank("proj0"), bank("proj1")]
        sc = [bank("scores0"), bank("scores1")]
        att = bank("att")
        matt = bank("mem_att")

        small_in = sem("small_in")
        mask_in = sem("mask_in")
        gain_mem_in = sem("gain_mem_in")
        gain_mix_in = sem("gain_mix_in")
        w_mem_in = sem("w_mem_in")
        early_in = [sem("mem0_in"), sem("mem1_in"), sem("x0_in")]
        x_in = sem("x_in")
        stage_in = [sem(f"stage{j}_in") for j in range(4)]
        mix_out = sem("mix_out")
        prepared = sem("prepared")
        sinks_set = sem("sinks_set")
        cleared = sem("cleared")
        wh_ready = sem("wh_ready")
        wl_ready = sem("wl_ready")
        xy_ready = sem("xy_ready")
        xr_ready = sem("xr_ready")
        xs_ready = sem("xs_ready")
        x_turned = sem("x_turned")
        xh_ready = sem("xh_ready")
        xl_ready = sem("xl_ready")
        memT_ready = sem("memT_ready")
        kv_done = sem("kv_done")
        kv_taken = sem("kv_taken")
        q_squared = sem("q_squared")
        qss_ready = sem("qss_ready")
        qy_ready = sem("qy_ready")
        qn_ready = sem("qn_ready")
        km_turned = sem("km_turned")
        km_ready = sem("km_ready")
        proj_done = sem("proj_done")
        proj_taken = sem("proj_taken")
        q_turned = sem("q_turned")
        qT_ready = sem("qT_ready")
        k_shifted = sem("k_shifted")
        v_shifted = sem("v_shifted")
        u_ready = sem("u_ready")
        hist_ready = sem("hist_ready")
        conv_turned = sem("conv_turned")
        convT_ready = sem("convT_ready")
        scores_done = sem("scores_done")
        max_ready = sem("max_ready")
        exp_ready = sem("exp_ready")
        probs_ready = sem("probs_ready")
        p_turned = sem("p_turned")
        pT_ready = sem("pT_ready")
        pv_done = sem("pv_done")
        mpv_done = sem("mpv_done")
        mix_parts = sem("mix_parts")
        mix_squared = sem("mix_squared")
        stats_done = sem("stats_done")
        stats_taken = sem("stats_taken")
        act_x, act_q = sem("act_x"), sem("act_q")
        pool_x, pool_q, pool_v, pool_s = sem("pool_x"), sem("pool_q"), sem("pool_v"), sem("pool_s")
        dve_max, dve_sum, dve_conv = sem("dve_max"), sem("dve_sum"), sem("dve_conv")

        block = ctx.enter_context(nc.Block())

        @block.sync
        def _(sp):
            sp.dma_start(early[0], mem[0]).then_inc(early_in[0], 16)
            sp.dma_start(gain[:, :], gain_mem).then_inc(gain_mem_in, 16)
            sp.dma_start(region[:, 0:DC * 2 * MEM_W], w_mem).then_inc(w_mem_in, 16)
            for c in range(3):
                sp.dma_start(stage[c], w_in[:, c, :]).then_inc(stage_in[c], 16)
            sp.wait_ge(xs_ready, 2)
            sp.dma_start(gain[:, :], gain_mix).then_inc(gain_mix_in, 16)
            sp.dma_start(stage[3], w_in[:, 3, :]).then_inc(stage_in[3], 16)
            for c in range(4, DC):
                sp.wait_ge(wl_ready, c - 3)
                sp.dma_start(stage[c % 4], w_in[:, c, :]).then_inc(stage_in[c % 4], 16)
            sp.dma_start(xt[:, :], x[1]).then_inc(x_in, 16)
            sp.wait_ge(wl_ready, DC)
            sp.dma_start(mask[:, :, :], masks).then_inc(mask_in, 16)

            def store(t):
                sp.wait_ge(mix_parts, 3 * t + 3)
                sp.dma_start(mixed[t], region2[:, D:2 * D]).then_inc(mix_out, 16)

            with sp.Fori(0, TILES - 2) as t:
                sp.wait_ge(xs_ready, t + 4)
                sp.dma_start(xt[:, :], x[t + 2]).then_inc(x_in, 16)
                store(t)
            store(TILES - 2)
            store(TILES - 1)
            sp.wait_ge(mix_out, 16 * TILES)

        @block.tensor
        def _(pe):
            def turn_x(i):
                pe.wait_ge(xs_ready, i + 1)
                for b in range(2):
                    for c in range(4):
                        last = pe.transpose(turn[b][:, c * P:(c + 1) * P], xs[:, (4 * b + c) * P:(4 * b + c + 1) * P],
                                            ident[:, :])
                    last.then_inc(x_turned, 1)

            def project(g, first=False):
                cols_g = slice(g * GROUP, (g + 1) * GROUP)
                for c in range(DC):
                    if first:
                        pe.wait_ge(wl_ready, c + 1)
                    last = three_passes(pe, proj[g % 2][:, 0:GROUP], xh[:, c, :], xl[:, c, :],
                                        wh[:, c, cols_g], wl[:, c, cols_g], c == 0, c == DC - 1)
                last.then_inc(proj_done, 1)

            def scores_of(u):
                for n in range(2):
                    rows = unit_rows(u)
                    if u < 4:
                        q, keys = qT[rows, 2 * (u // 2) + n, :], kT[rows, :]
                    else:
                        q, keys = mqT[rows, n, :], kmT[rows, n, :]
                    last = pe.matmul(sc[u % 2][:, n * KEYS:(n + 1) * KEYS], q, keys, start=True, stop=True)
                last.then_inc(scores_done, 1)

            def turn_probs(t, u):
                pe.wait_ge(probs_ready, UNITS * t + u + 1)
                to = turn[(u + 1) % 2]
                for b in range(2):
                    for n in range(2):
                        last = pe.transpose(to[:, (2 * b + n) * P:(2 * b + n + 1) * P],
                                            probs[:, unit_heads(u) + n, b * P:(b + 1) * P], ident[:, :])
                last.then_inc(p_turned, 1)

            def turn_qk(t):
                pe.wait_ge(qn_ready, t + 3)
                for c in range(4):
                    last = pe.transpose(turn[1][:, c * P:(c + 1) * P], pq[:, c * P:(c + 1) * P], ident[:, :])
                last.then_inc(q_turned, 1)
                for c in range(3):
                    last = pe.transpose(turn[0][:, c * P:(c + 1) * P], pq[:, (4 + c) * P:(5 + c) * P], ident[:, :])
                last.then_inc(q_turned, 1)

            def turn_conv():
                for j, col in enumerate((C0, C0 + P, B0, B0 + P)):
                    last = pe.transpose(turn[0][:, j * P:(j + 1) * P], pv[:, col:col + P], ident[:, :])
                last.then_inc(conv_turned, 1)

            def mean_squares(t):
                pe.wait_ge(mix_squared, t + 1)
                for j, chunks in enumerate(GROUP_CHUNKS):
                    last = pe.matmul(matt[:, j:j + 1], sqmix[:, chunks[0], :], small[:, MEANS + j:MEANS + j + 1],
                                     start=True, stop=True)
                last.then_inc(stats_done, 1)

            def window_attention():
                for g in range(2):
                    rows = slice(HD * g, HD * g + HD)
                    for b in range(2):
                        last = pe.matmul(att[rows, :], v2[:, b, rows], pT[:, b, 4 * g:4 * g + 4, :],
                                         start=(b == 0), stop=(b == 1))
                last.then_inc(pv_done, 1)

            def memory_attention():
                for e in range(2):
                    rows = slice(HD * e, HD * e + HD)
                    for c in range(2):
                        head = slice(HD * (2 * c + e), HD * (2 * c + e) + HD)
                        for b in range(2):
                            last = pe.matmul(matt[rows, c * P:(c + 1) * P], vm[:, b, head], mpT[:, b, 2 * e + c, :],
                                             start=(b == 0), stop=(b == 1))
                last.then_inc(mpv_done, 1)

            def tile(t, first=False, final=False):
                nxt = t + 1

                def project_next(g):
                    if not final:
                        pe.wait_ge(proj_taken, GROUPS * nxt + g - 1)
                        project(g)

                pe.wait_ge(qT_ready, 3 * t + 3)
                if not final:
                    turn_x(nxt + 2)
                if not first:
                    pe.wait_ge(exp_ready, UNITS * t - 1)
                scores_of(0)
                if not first:
                    pe.wait_ge(exp_ready, UNITS * t)
                scores_of(1)
                pe.wait_ge(u_ready, t + 1)
                if not final:
                    pe.wait_ge(xl_ready, 2 * nxt + 1)
                turn_conv()
                if not final:
                    pe.wait_ge(xl_ready, 2 * nxt + 2)
                project_next(0)
                pe.wait_ge(max_ready, UNITS * t + 1)
                scores_of(2)
                turn_probs(t, 0)
                if not first:
                    mean_squares(t - 1)
                project_next(1)
                pe.wait_ge(max_ready, UNITS * t + 2)
                scores_of(3)
                pe.wait_ge(convT_ready, t + 1)
                turn_probs(t, 1)
                pe.wait_ge(max_ready, UNITS * t + 3)
                scores_of(4)
                pe.wait_ge(pT_ready, UNITS * t + 1)
                turn_probs(t, 2)
                project_next(2)
                pe.wait_ge(max_ready, UNITS * t + 4)
                scores_of(5)
                pe.wait_ge(pT_ready, UNITS * t + 2)
                turn_probs(t, 3)
                project_next(3)
                pe.wait_ge(pT_ready, UNITS * t + 3)
                turn_probs(t, 4)
                pe.wait_ge(pT_ready, UNITS * t + 4)
                turn_probs(t, 5)
                pe.wait_ge(v_shifted, t + 1)
                if not first:
                    pe.wait_ge(mix_parts, 3 * t)
                window_attention()
                pe.wait_ge(pT_ready, UNITS * t + 6)
                if not final:
                    turn_qk(nxt)
                if not first:
                    pe.wait_ge(stats_taken, t)
                memory_attention()

            pe.wait_ge(small_in, 32)
            def turn_km(m):
                pe.wait_ge(qn_ready, m + 1)
                for c in range(2):
                    last = pe.transpose(turn[0][:, c * P:(c + 1) * P], km[m][:, c * P:(c + 1) * P], ident[:, :])
                last.then_inc(km_turned, 1)

            for m in range(2):
                turn_x(m)
                if m == 0:
                    pe.wait_ge(w_mem_in, 16)
                pe.wait_ge(memT_ready, m + 1)
                for c in range(DC):
                    last = pe.matmul(proj[m][:, :], memT[:, c, :], w_mem_sb[:, c, :], start=(c == 0), stop=(c == DC - 1))
                last.then_inc(kv_done, 1)
            turn_x(2)
            pe.wait_ge(xl_ready, 2)
            turn_km(0)
            pe.wait_ge(kv_taken, 2)
            project(0, first=True)
            pe.wait_ge(km_ready, 1)
            turn_km(1)
            for g in range(1, GROUPS):
                if g > 1:
                    pe.wait_ge(proj_taken, g - 1)
                project(g)
            pe.wait_ge(km_ready, 2)
            turn_qk(0)
            tile(0, first=True)
            with pe.Fori(1, TILES - 1) as t:
                tile(t)
            tile(TILES - 1, final=True)
            mean_squares(TILES - 1)

        @block.scalar
        def _(act):
            x_steps = Steps(act, act_x, 3)
            q_steps = Steps(act, act_q, 2)

            def x_rstd(i, before=None):
                if before is not None:
                    act.wait_ge(early_in[i], 16)
                else:
                    act.wait_ge(x_in, 16 * i - 32)
                if before is None or i:
                    act.wait_ge(x_turned, 2 * i)
                x_steps.start(i)
                x_steps.then_wait(act.activation(xs[:, :], xt[:, :] if before is None else before, ACT.Square,
                                                 accum_out=ssq[:, :]))
                x_steps.then_wait(act.activation(xv[:, :], ssq[:, :], ACT.Identity, bias=small[:, EPS4:EPS4 + 1],
                                                 scale=4.0 / D))
                rsqrt_table(act, x_steps, xr[:, :], xln[:, :], xv[:, :]).then_inc(xy_ready, 1)

            def q_rstd(i, n=QK_HEADS):
                act.wait_ge(qss_ready, i + 1)
                q_steps.start(i)
                q_steps.then_wait(act.activation(qv[:, 0:n], qss[:, 0:n], ACT.Identity, bias=small[:, EPS4:EPS4 + 1],
                                                 scale=4.0 / HD))
                rsqrt_table(act, q_steps, qr[:, 0:n], qln[:, 0:n], qv[:, 0:n]).then_inc(qy_ready, 1)

            def split_x(t):
                for b in range(2):
                    act.wait_ge(x_turned, 2 * t + 4 + b + 1)
                    act.activation(xh[:, 4 * b:4 * b + 4, :], turn[b][:, :], ACT.Copy).then_inc(xh_ready, 1)

            def take_proj(t, g, first=False):
                act.wait_ge(proj_done, GROUPS * t + g + 1)
                if g == 2 and not first:
                    act.wait_ge(v_shifted, t)
                to = pq if g < 2 else pv
                act.activation(to[:, (g % 2) * GROUP:(g % 2 + 1) * GROUP], proj[g % 2][:, 0:GROUP],
                               ACT.Copy).then_inc(proj_taken, 1)

            def take_qT(t):
                act.wait_ge(q_turned, 2 * t + 1)
                act.activation(qT[:, :, :], turn[1][:, :], ACT.Copy, scale=q8[:, 0:1]).then_inc(qT_ready, 1)
                act.wait_ge(q_turned, 2 * t + 2)
                act.wait_ge(k_shifted, t + 1)
                act.activation(kT[:, P:KEYS], turn[0][:, 0:P], ACT.Copy, scale=small[:, KG:KG + 1]).then_inc(qT_ready, 1)
                act.activation(mqT[:, :, :], turn[0][:, P:3 * P], ACT.Copy, scale=q8[:, 1:2]).then_inc(qT_ready, 1)

            def take_convT(t):
                act.wait_ge(conv_turned, t + 1)
                act.wait_ge(hist_ready, t + 1)
                act.activation(uT[:, :, 2:P + 2], turn[0][:, 0:CONV_CH].rearrange("p (c q) -> p c q", c=CC), ACT.Copy)
                act.activation(bT[:, :, :], turn[0][:, CONV_CH:2 * CONV_CH].rearrange("p (c q) -> p c q", c=CC),
                               ACT.Copy).then_inc(convT_ready, 1)

            def exps(t, u, first=False):
                act.wait_ge(max_ready, UNITS * t + u + 1)
                if first:
                    act.wait_ge(cleared, 1)
                    act.wait_ge(sinks_set, 1)
                else:
                    act.wait_ge(p_turned, UNITS * (t - 1) + u + 1)
                lo = P if first else 0
                for n in range(2):
                    h = unit_heads(u) + n
                    if u < 4:
                        out, of = probs[:, h, lo:KEYS + 1], scores[:, h, lo:KEYS + 1]
                    else:
                        out, of = probs[:, h, 0:KEYS], sc[u % 2][:, n * KEYS:(n + 1) * KEYS]
                    last = act.activation(out, of, ACT.Exp, bias=nm[:, h:h + 1], accum_out=rs[:, h:h + 1])
                last.then_inc(exp_ready, 1)

            def take_pT(t, u, first=False):
                act.wait_ge(p_turned, UNITS * t + u + 1)
                if not first:
                    act.wait_ge(pv_done if u < 4 else mpv_done, t)
                h = unit_heads(u)
                to = pT[:, :, h:h + 2, :] if u < 4 else mpT[:, :, h - 8:h - 6, :]
                act.activation(to, turn[(u + 1) % 2][:, :].rearrange("p (b h q) -> p b h q", b=2, h=2),
                               ACT.Copy).then_inc(pT_ready, 1)

            def split_w(c):
                act.wait_ge(stage_in[c % 4], 16 * (c // 4 + 1))
                act.activation(wh[:, c, :], stage[c % 4], ACT.Copy).then_inc(wh_ready, 1)

            def tile(t, first=False, norm=True, final=False):
                nxt = t + 1
                if not final:
                    split_x(nxt)
                exps(t, 0, first)
                exps(t, 1, first)
                if norm:
                    x_rstd(t + 4)
                take_convT(t)
                if not final:
                    take_proj(nxt, 0)
                exps(t, 2, first)
                take_pT(t, 0, first)
                if not final:
                    take_proj(nxt, 1)
                exps(t, 3, first)
                take_pT(t, 1, first)
                exps(t, 4, first)
                take_pT(t, 2, first)
                if not final:
                    take_proj(nxt, 2)
                    q_rstd(nxt + 2)
                exps(t, 5, first)
                take_pT(t, 3, first)
                if not final:
                    take_proj(nxt, 3)
                take_pT(t, 4, first)
                take_pT(t, 5, first)
                if not final:
                    take_qT(nxt)

            def take_memT(m):
                for b in range(2):
                    act.wait_ge(x_turned, 2 * m + b + 1)
                    last = act.activation(memT[:, 4 * b:4 * b + 4, :], turn[b][:, :], ACT.Copy)
                last.then_inc(memT_ready, 1)

            def take_kv(m):
                act.wait_ge(kv_done, m + 1)
                act.activation(km[m], proj[m][:, 0:MEM_W], ACT.Copy)
                act.activation(vm[:, m, :], proj[m][:, MEM_W:2 * MEM_W], ACT.Copy).then_inc(kv_taken, 1)

            def take_kmT(m):
                act.wait_ge(km_turned, m + 1)
                act.activation(kmT[:, :, m * P:(m + 1) * P], turn[0][:, 0:2 * P].rearrange("p (c q) -> p c q", c=2),
                               ACT.Copy, scale=small[:, MKG:MKG + 1]).then_inc(km_ready, 1)

            act.dma_start(small[:, :], cols).then_inc(small_in, 16)
            act.dma_start(ident[:, :], ident_d).then_inc(small_in, 16)
            act.dma_start(early[1], mem[1]).then_inc(early_in[1], 16)
            act.dma_start(early[2], x[0]).then_inc(early_in[2], 16)
            act.preload_act_table_set(ACT_SET)
            act.wait_ge(small_in, 32)
            x_rstd(0, early[0])
            take_memT(0)
            x_rstd(1, early[1])
            split_w(0)
            take_memT(1)
            x_rstd(2, early[2])
            take_kv(0)
            split_w(1)
            split_w(2)
            take_kv(1)
            q_rstd(0, MEM_HEADS)
            split_x(0)
            split_w(3)
            take_kmT(0)
            split_w(4)
            q_rstd(1, MEM_HEADS)
            for c in range(5, DC):
                split_w(c)
            x_rstd(3)
            take_proj(0, 0, first=True)
            take_kmT(1)
            for g in range(1, GROUPS):
                take_proj(0, g, first=True)
                if g == 2:
                    q_rstd(2)
            act.wait_ge(prepared, 1)
            take_qT(0)
            tile(0, first=True)
            with act.Fori(1, TILES - 2) as t:
                tile(t)
            tile(TILES - 2, norm=False)
            tile(TILES - 1, norm=False, final=True)

        @block.vector
        def _(dve):
            max_steps = Steps(dve, dve_max, 2 * 4 + 2)
            sum_steps = Steps(dve, dve_sum, UNITS)
            conv_steps = Steps(dve, dve_conv, 3)

            def scale_x(i, of=xt[:, :]):
                dve.wait_ge(xr_ready, i + 1)
                dve.scalar_tensor_tensor(out=xs[:, :], in0=of, scalar=xr[:, 0:1], in1=gain[:, :],
                                         op0=ALU.mult, op1=ALU.mult).then_inc(xs_ready, 1)

            def low_x(t):
                for b in range(2):
                    dve.wait_ge(xh_ready, 2 * t + b + 1)
                    dve.tensor_tensor(xl[:, 4 * b:4 * b + 4, :], turn[b][:, :].rearrange("p (c q) -> p c q", c=4),
                                      xh[:, 4 * b:4 * b + 4, :], ALU.subtract).then_inc(xl_ready, 1)

            def low_w(c):
                dve.wait_ge(wh_ready, c + 1)
                dve.tensor_tensor(wl[:, c, :], stage[c % 4], wh[:, c, :], ALU.subtract).then_inc(wl_ready, 1)

            def head_sums(i, of, n=QK_HEADS):
                dve.wait_ge(q_squared, i + 1)
                dve.tensor_reduce(qss[:, 0:n], of.rearrange("p (h d) -> p h d", d=HD), AX_X, ALU.add).then_inc(qss_ready, 1)

            def maxima(t, u, first=False):
                if not first:
                    dve.wait_ge(exp_ready, UNITS * (t - 1) + u + 1)
                dve.wait_ge(scores_done, UNITS * t + u + 1)
                h0 = unit_heads(u)
                if u < 4:
                    lo = P if first else 0
                    biased = scores[:, h0:h0 + 2, lo:KEYS]
                    of = sc[u % 2][:, :].rearrange("p (n k) -> p n k", n=2)[:, :, lo:KEYS]
                    max_steps.then_wait(dve.tensor_tensor(biased, of, mask[:, h0:h0 + 2, lo:KEYS], ALU.add))
                    max_steps.then_wait(dve.tensor_reduce(mx[:, h0:h0 + 2], biased, AX_X, ALU.max))
                    dve.scalar_tensor_tensor(out=nm[:, h0:h0 + 2], in0=mx[:, h0:h0 + 2], scalar=-1.0,
                                             in1=neg_sink[:, h0:h0 + 2], op0=ALU.mult, op1=ALU.min).then_inc(max_ready, 1)
                else:
                    max_steps.then_wait(dve.tensor_reduce(mx[:, h0:h0 + 2], sc[u % 2][:, :].rearrange("p (n k) -> p n k", n=2),
                                                          AX_X, ALU.max))
                    dve.tensor_scalar(nm[:, h0:h0 + 2], mx[:, h0:h0 + 2], -1.0, None, ALU.mult).then_inc(max_ready, 1)

            def divide(t, u):
                dve.wait_ge(exp_ready, UNITS * t + u + 1)
                h0 = unit_heads(u)
                sum_steps.then_wait(dve.reciprocal(rr[:, h0:h0 + 2], rs[:, h0:h0 + 2]))
                for h in (h0, h0 + 1):
                    last = dve.tensor_scalar(probs[:, h, 0:KEYS], probs[:, h, 0:KEYS], rr[:, h:h + 1], None, ALU.mult)
                last.then_inc(probs_ready, 1)

            def convolve(t, first=False):
                dve.wait_ge(convT_ready, t + 1)
                if not first:
                    dve.wait_ge(mix_out, 16 * t)
                    dve.wait_ge(mix_squared, t)
                conv_steps.start(t)
                for c in range(CC):
                    last = dve.tensor_scalar(cy[:, c, :], uT[:, c, 0:P], small[:, CW + 3 * c:CW + 3 * c + 1], None, ALU.mult)
                conv_steps.then_wait(last)
                for j in (1, 2):
                    for c in range(CC):
                        w = small[:, CW + 3 * c + j:CW + 3 * c + j + 1]
                        last = dve.scalar_tensor_tensor(out=cy[:, c, :], in0=uT[:, c, j:j + P], scalar=w, in1=cy[:, c, :],
                                                        op0=ALU.mult, op1=ALU.add)
                    conv_steps.then_wait(last)
                for c in range(CC):
                    last = dve.scalar_tensor_tensor(out=mix[:, 4 + c, :], in0=cy[:, c, :], scalar=small[:, CB + c:CB + c + 1],
                                                    in1=bT[:, c, :], op0=ALU.add, op1=ALU.mult)
                last.then_inc(mix_parts, 1)

            def take_attention(t):
                dve.wait_ge(pv_done, t + 1)
                dve.tensor_copy(region2[:, D:D + 4 * P], att[:, :]).then_inc(mix_parts, 1)
                dve.wait_ge(mpv_done, t + 1)
                dve.tensor_copy(region2[:, D + 6 * P:D + 8 * P], matt[:, 0:2 * P]).then_inc(mix_parts, 1)

            def take_stats(t):
                dve.wait_ge(stats_done, t + 1)
                dve.tensor_scalar(stats[:, t, :], matt[:, 0:3], 4 * EPS, None, ALU.add).then_inc(stats_taken, 1)

            def tile(t, first=False, norm=True, final=False):
                nxt = t + 1
                max_steps.start(t)
                sum_steps.start(t)
                if not final:
                    low_x(nxt)
                maxima(t, 0, first)
                maxima(t, 1, first)
                divide(t, 0)
                if not first:
                    take_stats(t - 1)
                maxima(t, 2, first)
                divide(t, 1)
                if norm:
                    scale_x(t + 4)
                divide(t, 2)
                maxima(t, 3, first)
                if not final:
                    head_sums(nxt + 2, squares[:, 0:QK])
                maxima(t, 4, first)
                divide(t, 3)
                maxima(t, 5, first)
                divide(t, 4)
                convolve(t, first)
                divide(t, 5)
                take_attention(t)

            dve.wait_ge(gain_mem_in, 16)
            scale_x(0, early[0])
            scale_x(1, early[1])
            low_w(0)
            dve.wait_ge(gain_mix_in, 16)
            scale_x(2, early[2])
            low_w(1)
            low_w(2)
            head_sums(0, km_sq[:, :], MEM_HEADS)
            low_x(0)
            low_w(3)
            head_sums(1, km_sq[:, :], MEM_HEADS)
            for c in range(4, DC):
                low_w(c)
            scale_x(3)
            head_sums(2, squares[:, 0:QK])
            dve.wait_ge(mask_in, 16)
            dve.wait_ge(prepared, 1)
            tile(0, first=True)
            with dve.Fori(1, TILES - 2) as t:
                tile(t)
            tile(TILES - 2, norm=False)
            tile(TILES - 1, norm=False, final=True)
            take_stats(TILES - 1)

        @block.gpsimd
        def _(pool):
            x_steps = Steps(pool, pool_x, 3)
            q_steps = Steps(pool, pool_q, 4)
            v_steps = Steps(pool, pool_v, 1)
            s_steps = Steps(pool, pool_s, 2)

            def copy(to, of):
                one = small[:, ONE:ONE + 1]
                if len(of.shape) == 3:
                    one = one.unsqueeze(2)
                return pool.tensor_tensor(to, of, one.to_broadcast(list(of.shape)), ALU.mult)

            def x_newton(i):
                pool.wait_ge(xy_ready, i + 1)
                x_steps.start(i)
                rsqrt_newton(pool, x_steps, xr[:, :], xv[:, :], xn2[:, :], small[:, THREE:THREE + 1]).then_inc(xr_ready, 1)

            def q_square(i, out, of):
                pool.tensor_tensor(out, of, of, ALU.mult).then_inc(q_squared, 1)

            def q_norm(i, of, n=QK_HEADS):
                pool.wait_ge(qy_ready, i + 1)
                q_steps.start(i)
                three = small[:, THREE:THREE + 1].to_broadcast([P, n])
                q_steps.then_wait(rsqrt_newton(pool, q_steps, qr[:, 0:n], qv[:, 0:n], qn2[:, 0:n], three))
                heads = of.rearrange("p (h d) -> p h d", d=HD)
                by = qr[:, 0:n].unsqueeze(2).to_broadcast([P, n, HD])
                pool.tensor_tensor(heads, heads, by, ALU.mult).then_inc(qn_ready, 1)

            def square_proj(t, wait_stats=True):
                pool.wait_ge(proj_taken, GROUPS * t + 2)
                if wait_stats:
                    pool.wait_ge(stats_done, t - 1)
                q_square(t + 2, squares[:, 0:QK], pq[:, :])

            def shift_k(t):
                pool.wait_ge(scores_done, UNITS * (t - 1) + 4)
                copy(kT[:, 0:P], kT[:, P:KEYS]).then_inc(k_shifted, 1)

            def shift_v(t, first=False):
                if first:
                    v_steps.start(t)
                    v_steps.then_wait(pool.memset(v2[:, 0, :], 0.0))
                else:
                    pool.wait_ge(pv_done, t)
                    v_steps.start(t)
                    v_steps.then_wait(copy(v2[:, 0, :], v2[:, 1, :]))
                pool.wait_ge(proj_taken, GROUPS * t + 3)
                copy(v2[:, 1, :], pv[:, V0:V0 + P]).then_inc(v_shifted, 1)

            def gate(t):
                pool.wait_ge(proj_taken, GROUPS * t + 4)
                pool.tensor_tensor(pv[:, C0:C0 + CONV_CH], pv[:, C0:C0 + CONV_CH], pv[:, H0:H0 + CONV_CH],
                                   ALU.mult).then_inc(u_ready, 1)

            def history(t):
                pool.wait_ge(mix_parts, 3 * t - 2)
                copy(uT[:, :, 0:2], uT[:, :, P:P + 2]).then_inc(hist_ready, 1)

            def square_mix(t):
                pool.wait_ge(mix_parts, 3 * t + 3)
                s_steps.start(t)
                s_steps.then_wait(pool.tensor_tensor(squares, region2[:, D:2 * D], region2[:, D:2 * D], ALU.mult))
                s_steps.then_wait(pool.tensor_tensor(sqmix[:, 0:2, :], sqmix[:, 0:2, :], sqmix[:, 2:4, :], ALU.add))
                pool.tensor_tensor(sqmix[:, 0:8:4, :], sqmix[:, 0:8:4, :], sqmix[:, 1:8:4, :], ALU.add)
                pool.tensor_tensor(sqmix[:, 6, :], sqmix[:, 6, :], sqmix[:, 7, :], ALU.add).then_inc(mix_squared, 1)

            def tile(t, first=False, norm=True, final=False):
                nxt = t + 1
                if not first:
                    square_mix(t - 1)
                if norm:
                    x_newton(t + 4)
                if final:
                    return
                square_proj(nxt, wait_stats=not first)
                shift_k(nxt)
                q_norm(nxt + 2, pq[:, :])
                history(nxt)
                gate(nxt)
                shift_v(nxt)

            pool.memset(uT[:, :, 0:2], 0.0).then_inc(hist_ready, 1)
            pool.memset(kT[:, 0:P], 0.0).then_inc(k_shifted, 1)
            pool.wait_ge(small_in, 32)
            pool.tensor_scalar(q8[:, 0:1], small[:, QG:QG + 1], HD ** -0.5, None, ALU.mult)
            pool.tensor_scalar(q8[:, 1:2], small[:, MQG:MQG + 1], HD ** -0.5, None, ALU.mult)
            pool.tensor_scalar(neg_sink[:, :], small[:, SINK:SINK + HEADS], -1.0, None, ALU.mult).then_inc(prepared, 1)
            for i in range(3):
                x_newton(i)
            for m in range(2):
                pool.wait_ge(kv_taken, m + 1)
                q_square(m, km_sq[:, :], km[m])
                q_norm(m, km[m], MEM_HEADS)
            pool.wait_ge(kv_done, 2)
            pool.memset(region[:, 0:HEADS * (KEYS + 1)], 0.0).then_inc(cleared, 1)
            pool.wait_ge(wl_ready, DC - 1)
            pool.tensor_copy(scores[:, :, KEYS], small[:, SINK:SINK + HEADS]).then_inc(sinks_set, 1)
            x_newton(3)
            square_proj(0, wait_stats=False)
            q_norm(2, pq[:, :])
            gate(0)
            shift_v(0, first=True)
            tile(0, first=True)
            with pool.Fori(1, TILES - 2) as t:
                tile(t)
            tile(TILES - 2, norm=False)
            tile(TILES - 1, norm=False, final=True)
            square_mix(TILES - 1)


def out_phase(nc, half, x, mixed, w_out, out_gain, gain_ffn, ident_d, rall, y, xh, xl):
    with ExitStack() as ctx:
        def sb(name, shape, dt=F32):
            return ctx.enter_context(nc.sbuf_tensor(f"{name}_{half}", shape, dt))

        def sem(name):
            return ctx.enter_context(nc.semaphore(f"{name}_{half}"))

        wh = sb("w_out_high", [P, DC, D], F32R)
        wl = sb("w_out_low", [P, DC, D], F32R)
        stage = sb("w_out_stage", [P, 2, D])
        gains = sb("out_gains", [P, DC])
        gain = sb("gain_ffn_row", [P, D])
        ident = sb("ident_out", [P, P])
        mt = sb("mixed_tile", [P, 2, D])
        mh = [sb(f"mixed_high{s}", [P, DC, P], F32R) for s in range(2)]
        ml = [sb(f"mixed_low{s}", [P, DC, P], F32R) for s in range(2)]
        ys = sb("y_normed", [P, D])
        ssq = sb("y_ssq", [P, 1])
        yv = sb("y_var", [P, 1])
        yln = sb("y_ln", [P, 1])
        yr = sb("y_rstd", [P, 1])
        yn2 = sb("y_newton", [P, 1])
        eps4 = sb("eps4", [P, 1])
        three = sb("three", [P, 1])

        def bank(name):
            return ctx.enter_context(nc.psum_tensor(f"{name}_{half}", [P, BANK], F32))

        turn = [bank("y_turn0"), bank("y_turn1")]
        parts = [[bank(f"out{n}_{g}") for g in range(3)] for n in range(2)]

        small_in = sem("o_small_in")
        stage_in = [sem("o_stage0_in"), sem("o_stage1_in")]
        y_in = sem("y_in")
        mt_in = [sem("mt0_in"), sem("mt1_in")]
        wh_ready = sem("o_wh_ready")
        wl_ready = sem("o_wl_ready")
        mh_ready = sem("mh_ready")
        ml_ready = sem("ml_ready")
        out_done = sem("out_done")
        y_ready = sem("y_ready")
        consts_set = sem("consts_set")
        yy_ready = sem("yy_ready")
        yr_ready = sem("yr_ready")
        ys_ready = sem("ys_ready")
        y_turned = sem("y_turned")
        yh_ready = sem("yh_ready")
        yl_ready = sem("yl_ready")
        act_y, pool_y, dve_y = sem("act_y"), sem("pool_y"), sem("dve_y")

        block = ctx.enter_context(nc.Block())
        first_tile = half * HT

        @block.sync
        def _(sp):
            sp.dma_start(gains[:, :], out_gain).then_inc(small_in, 16)
            for c in range(2):
                sp.dma_start(stage[:, c, :], w_out[:, c, :]).then_inc(stage_in[c], 16)
            sp.dma_start(ident[:, :], ident_d).then_inc(small_in, 16)
            sp.dma_start(gain[:, :], gain_ffn).then_inc(small_in, 16)
            for j in range(2):
                sp.dma_start(mt[:, j, :], mixed[first_tile + j]).then_inc(mt_in[j], 16)
            for c in range(2, DC):
                sp.wait_ge(wl_ready, c - 1)
                sp.dma_start(stage[:, c % 2, :], w_out[:, c, :]).then_inc(stage_in[c % 2], 16)
            sp.dma_start(y[:, :, :], x[first_tile:first_tile + HT].rearrange("t p d -> p t d")).then_inc(y_in, 16)
            with sp.Fori(1, HT // 2) as k:
                for j in range(2):
                    sp.wait_ge(ml_ready, 2 * k + j - 1)
                    sp.dma_start(mt[:, j, :], mixed[2 * k + (first_tile + j)]).then_inc(mt_in[j], 16)

        @block.tensor
        def _(pe):
            def project(slot, n):
                for g, chunks in enumerate(GROUP_CHUNKS):
                    for c in chunks:
                        last = three_passes(pe, parts[n][g][:, :], mh[slot][:, c, :], ml[slot][:, c, :],
                                            wh[:, c, n * BANK:(n + 1) * BANK], wl[:, c, n * BANK:(n + 1) * BANK],
                                            c == chunks[0], c == chunks[-1])
                last.then_inc(out_done, 1)

            def turn_y(j, first=False):
                pe.wait_ge(ys_ready, j + 1)
                for b in range(2):
                    if not first:
                        pe.wait_ge(yl_ready, 2 * j + b - 1)
                    for c in range(4):
                        last = pe.transpose(turn[b][:, c * P:(c + 1) * P], ys[:, (4 * b + c) * P:(4 * b + c + 1) * P],
                                            ident[:, :])
                    last.then_inc(y_turned, 1)

            pe.wait_ge(small_in, 48)
            pe.wait_ge(ml_ready, 1)
            pe.wait_ge(wl_ready, DC)
            for n in range(2):
                project(0, n)

            def tile(j, slot, first=False):
                pe.wait_ge(ml_ready, j + 1)
                for n in range(2):
                    pe.wait_ge(y_ready, 2 * j + n - 1)
                    project(slot, n)
                turn_y(j - 1, first)

            tile(1, 1, first=True)
            with pe.Fori(1, HT // 2) as k:
                tile(2 * k, 0)
                tile(2 * k + 1, 1)
            turn_y(HT - 1)

        @block.scalar
        def _(act):
            y_steps = Steps(act, act_y, 3)

            def high_mixed(j, slot, first=False):
                act.wait_ge(mt_in[slot], 8 * (j - slot) + 16)
                if not first:
                    act.wait_ge(out_done, 2 * j - 2)
                act.activation(mh[slot][:, :, :], mt[:, slot, :], ACT.Copy).then_inc(mh_ready, 1)

            def y_rstd(j, first=False):
                act.wait_ge(y_ready, 2 * j + 2)
                if not first:
                    act.wait_ge(y_turned, 2 * j)
                y_steps.start(j)
                y_steps.then_wait(act.activation(ys[:, :], y[:, j, :], ACT.Square, accum_out=ssq[:, :]))
                y_steps.then_wait(act.activation(yv[:, :], ssq[:, :], ACT.Identity, bias=eps4[:, :], scale=4.0 / D))
                rsqrt_table(act, y_steps, yr[:, :], yln[:, :], yv[:, :]).then_inc(yy_ready, 1)

            def high_y(j):
                for b in range(2):
                    act.wait_ge(y_turned, 2 * j + b + 1)
                    act.activation(xh[:, 4 * b:4 * b + 4, bass.ts(j, P)],
                                   turn[b][:, :].rearrange("p (c q) -> p c q", c=4), ACT.Copy).then_inc(yh_ready, 1)

            act.preload_act_table_set(ACT_SET)
            act.wait_ge(small_in, 48)
            act.wait_ge(consts_set, 1)
            for c in range(DC):
                act.wait_ge(stage_in[c % 2], 16 * (c // 2 + 1))
                act.activation(wh[:, c, :], stage[:, c % 2, :], ACT.Copy, scale=gains[:, c:c + 1]).then_inc(wh_ready, 1)
                if c == 1:
                    high_mixed(0, 0, first=True)
            high_mixed(1, 1, first=True)
            for j in range(HT):
                if j + 2 < HT:
                    high_mixed(j + 2, j % 2)
                y_rstd(j, first=(j == 0))
                high_y(j)

        @block.vector
        def _(dve):
            y_steps = Steps(dve, dve_y, 4)

            def add_groups(j, t):
                for n in range(2):
                    dve.wait_ge(out_done, 2 * j + n + 1)
                    yn = y[:, j, n * BANK:(n + 1) * BANK]
                    for g in range(3):
                        ins = dve.scalar_tensor_tensor(out=yn, in0=parts[n][g][:, :], scalar=rall[:, t, g:g + 1], in1=yn,
                                                       op0=ALU.mult, op1=ALU.add)
                        if g < 2:
                            y_steps.then_wait(ins)
                    ins.then_inc(y_ready, 1)

            def scale_y(j):
                dve.wait_ge(yr_ready, j + 1)
                dve.scalar_tensor_tensor(out=ys[:, :], in0=y[:, j, :], scalar=yr[:, 0:1], in1=gain[:, :],
                                         op0=ALU.mult, op1=ALU.mult).then_inc(ys_ready, 1)

            def low_y(j):
                for b in range(2):
                    dve.wait_ge(yh_ready, 2 * j + b + 1)
                    part = slice(4 * b, 4 * b + 4)
                    dve.tensor_tensor(xl[:, part, bass.ts(j, P)], turn[b][:, :].rearrange("p (c q) -> p c q", c=4),
                                      xh[:, part, bass.ts(j, P)], ALU.subtract).then_inc(yl_ready, 1)

            dve.wait_ge(small_in, 48)
            for c in range(DC):
                dve.wait_ge(wh_ready, c + 1)
                dve.scalar_tensor_tensor(out=wl[:, c, :], in0=stage[:, c % 2, :], scalar=gains[:, c:c + 1], in1=wh[:, c, :],
                                         op0=ALU.mult, op1=ALU.subtract).then_inc(wl_ready, 1)
            dve.wait_ge(y_in, 16)
            for j in range(HT):
                y_steps.start(j)
                add_groups(j, first_tile + j)
                scale_y(j)
                if j:
                    low_y(j - 1)
            low_y(HT - 1)

        @block.gpsimd
        def _(pool):
            y_steps = Steps(pool, pool_y, 3)

            def low_mixed(j, slot, first=False):
                pool.wait_ge(mh_ready, j + 1)
                pool.tensor_tensor(ml[slot][:, :, :], mt[:, slot, :].rearrange("p (c q) -> p c q", c=DC), mh[slot][:, :, :],
                                   ALU.subtract).then_inc(ml_ready, 1)

            def y_norm(j):
                pool.wait_ge(yy_ready, j + 1)
                y_steps.start(j)
                rsqrt_newton(pool, y_steps, yr[:, :], yv[:, :], yn2[:, :], three[:, :]).then_inc(yr_ready, 1)

            pool.memset(three[:, :], 3.0)
            pool.memset(eps4[:, :], 4 * EPS).then_inc(consts_set, 1)
            pool.wait_ge(consts_set, 1)
            low_mixed(0, 0)
            low_mixed(1, 1)
            for j in range(HT):
                if j + 2 < HT:
                    low_mixed(j + 2, j % 2)
                y_norm(j)


def ffn_phase(nc, half, w_gu, w_down, out, y, xh, xl):
    with ExitStack() as ctx:
        def sb(name, shape, dt=F32):
            return ctx.enter_context(nc.sbuf_tensor(f"{name}_{half}", shape, dt))

        def sem(name):
            return ctx.enter_context(nc.semaphore(f"{name}_{half}"))

        gu_raw = sb("w_gu_raw", [P, 2, 2 * D])
        gu_h = sb("w_gu_high", [P, 2, 2 * D], F32R)
        gu_l = sb("w_gu_low", [P, 2, 2 * D], F32R)
        dn_raw = sb("w_down_raw", [P, 2 * D])
        dn_h = sb("w_down_high", [P, 2, D], F32R)
        dn_l = sb("w_down_low", [P, 2, D], F32R)
        hid_h = sb("hidden_high", [P, 2, 2, BANK], F32R)
        hid_l = sb("hidden_low", [P, 2, 2, BANK], F32R)
        act_g = sb("silu_gate", [P, BANK])
        hid = sb("hidden", [P, BANK])

        def bank(name):
            return ctx.enter_context(nc.psum_tensor(f"{name}_{half}", [P, BANK], F32))

        gate = [bank("gate0"), bank("gate1")]
        up = [bank("up0"), bank("up1")]
        down = [bank(f"down{k}") for k in range(4)]
        DOWNS = HT

        gu_in = [sem("gu0_in"), sem("gu1_in")]
        dn_in = sem("dn_in")
        guh_ready = sem("guh_ready")
        gul_ready = sem("gul_ready")
        dnh_ready = sem("dnh_ready")
        dnl_ready = sem("dnl_ready")
        gu_done = sem("gu_done")
        silu_ready = sem("silu_ready")
        hid_ready = sem("hid_ready")
        hh_ready = sem("hh_ready")
        hl_ready = sem("hl_ready")
        down_done = sem("down_done")
        y_added = sem("y_added")
        stored = sem("stored")

        block = ctx.enter_context(nc.Block())
        first_tile = half * HT

        @block.sync
        def _(sp):
            def load_gu(c, q):
                sp.dma_start(gu_raw[:, c, :], w_gu[q]).then_inc(gu_in[c], 16)

            load_gu(0, 0)
            load_gu(1, 1)
            sp.dma_start(dn_raw[:, :], w_down[0]).then_inc(dn_in, 16)
            with sp.Fori(1, PAIRS) as p:
                for c in range(2):
                    sp.wait_ge(gul_ready, 2 * p + c - 1)
                    load_gu(c, 2 * p + c)
                sp.wait_ge(dnl_ready, p)
                sp.dma_start(dn_raw[:, :], w_down[p]).then_inc(dn_in, 16)
            for k in range(HT):
                tb, j = k // 4, k % 4
                last = 2 * DOWNS * (PAIRS - 1) + DOWNS * tb + 2 * j + 2
                sp.wait_ge(y_added, last)
                sp.dma_start(out[first_tile + k], y[:, k, :]).then_inc(stored, 16)
            sp.wait_ge(stored, 16 * HT)

        @block.tensor
        def _(pe):
            def unit(p, tb, c, wait_banks=True):
                n = 2 * tb + c
                pe.wait_ge(gul_ready, 2 * p + c + 1)
                if wait_banks:
                    pe.wait_ge(hid_ready, 4 * p + n - 1)
                tokens = slice(tb * BANK, (tb + 1) * BANK)
                for k, to in enumerate((gate[c], up[c])):
                    for d in range(DC):
                        w = slice((k * DC + d) * P, (k * DC + d + 1) * P)
                        last = three_passes(pe, to[:, :], gu_h[:, c, w], gu_l[:, c, w], xh[:, d, tokens], xl[:, d, tokens],
                                            d == 0, d == DC - 1)
                last.then_inc(gu_done, 1)

            def down_block(p, tb, wait_banks=True):
                pe.wait_ge(dnl_ready, p + 1)
                pe.wait_ge(hl_ready, 4 * p + 2 * tb + 2)
                for g in range(DOWNS):
                    j, n = g // 2, g % 2
                    if wait_banks or g >= 4:
                        pe.wait_ge(y_added, 2 * DOWNS * p + DOWNS * tb + g - 3)
                    cols = slice(n * BANK, (n + 1) * BANK)
                    for c in range(2):
                        tok = slice(j * P, (j + 1) * P)
                        last = three_passes(pe, down[g % 4][:, :], hid_h[:, tb, c, tok], hid_l[:, tb, c, tok],
                                            dn_h[:, c, cols], dn_l[:, c, cols], c == 0, c == 1)
                    last.then_inc(down_done, 1)

            def pair(p, first=False):
                unit(p, 0, 0, wait_banks=not first)
                unit(p, 0, 1, wait_banks=not first)
                if not first:
                    down_block(p - 1, 1)
                unit(p, 1, 0)
                unit(p, 1, 1)
                down_block(p, 0, wait_banks=not first)

            pair(0, first=True)
            with pe.Fori(1, PAIRS) as p:
                pair(p)
            down_block(PAIRS - 1, 1)

        @block.scalar
        def _(act):
            def high_gu(p, c, first=False):
                act.wait_ge(gu_in[c], 16 * p + 16)
                if not first:
                    act.wait_ge(gu_done, 4 * p + c - 1)
                act.activation(gu_h[:, c, :], gu_raw[:, c, :], ACT.Copy).then_inc(guh_ready, 1)

            def high_down(p, first=False):
                act.wait_ge(dn_in, 16 * p + 16)
                if not first:
                    act.wait_ge(down_done, 2 * DOWNS * p)
                act.activation(dn_h[:, :, :], dn_raw[:, :].rearrange("p (c n) -> p c n", c=2), ACT.Copy).then_inc(dnh_ready, 1)

            def hidden(p, tb, c, first=False):
                n = 2 * tb + c
                act.wait_ge(gu_done, 4 * p + n + 1)
                if not first:
                    act.wait_ge(hid_ready, 4 * p + n)
                act.activation(act_g[:, :], gate[c][:, :], ACT.Silu).then_inc(silu_ready, 1)
                act.wait_ge(hid_ready, 4 * p + n + 1)
                act.activation(hid_h[:, tb, c, :], hid[:, :], ACT.Copy).then_inc(hh_ready, 1)

            def pair(p, first=False, final=False):
                hidden(p, 0, 0, first)
                hidden(p, 0, 1)
                if not first:
                    high_down(p)
                hidden(p, 1, 0)
                if not final:
                    high_gu(p + 1, 0)
                hidden(p, 1, 1)
                if not final:
                    high_gu(p + 1, 1)

            high_gu(0, 0, first=True)
            high_gu(0, 1, first=True)
            high_down(0, first=True)
            pair(0, first=True)
            with act.Fori(1, PAIRS - 1) as p:
                pair(p)
            pair(PAIRS - 1, final=True)

        @block.vector
        def _(dve):
            def low_gu(p, c):
                dve.wait_ge(guh_ready, 2 * p + c + 1)
                dve.tensor_tensor(gu_l[:, c, :], gu_raw[:, c, :], gu_h[:, c, :], ALU.subtract).then_inc(gul_ready, 1)

            def low_down(p):
                dve.wait_ge(dnh_ready, p + 1)
                dve.tensor_tensor(dn_l[:, :, :], dn_raw[:, :].rearrange("p (c n) -> p c n", c=2), dn_h[:, :, :],
                                  ALU.subtract).then_inc(dnl_ready, 1)

            def hidden(p, tb, c, first=False):
                n = 2 * tb + c
                dve.wait_ge(silu_ready, 4 * p + n + 1)
                if not first:
                    dve.wait_ge(hl_ready, 4 * p + n)
                dve.tensor_tensor(hid[:, :], up[c][:, :], act_g[:, :], ALU.mult).then_inc(hid_ready, 1)
                dve.wait_ge(hh_ready, 4 * p + n + 1)
                dve.tensor_tensor(hid_l[:, tb, c, :], hid[:, :], hid_h[:, tb, c, :], ALU.subtract).then_inc(hl_ready, 1)

            def add_down(p, tb):
                for g in range(DOWNS):
                    j, n = 4 * tb + g // 2, g % 2
                    dve.wait_ge(down_done, 2 * DOWNS * p + DOWNS * tb + g + 1)
                    yn = y[:, j, n * BANK:(n + 1) * BANK]
                    dve.tensor_tensor(yn, down[g % 4][:, :], yn, ALU.add).then_inc(y_added, 1)

            def pair(p, first=False, final=False):
                hidden(p, 0, 0, first)
                hidden(p, 0, 1)
                if not first:
                    add_down(p - 1, 1)
                    low_down(p)
                hidden(p, 1, 0)
                if not final:
                    low_gu(p + 1, 0)
                hidden(p, 1, 1)
                if not final:
                    low_gu(p + 1, 1)
                add_down(p, 0)

            low_gu(0, 0)
            low_gu(0, 1)
            low_down(0)
            pair(0, first=True)
            with dve.Fori(1, PAIRS - 1) as p:
                pair(p)
            pair(PAIRS - 1, final=True)
            add_down(PAIRS - 1, 1)


def group_rstds(nc, stats, rall, tmp, three):
    with (
        nc.semaphore("r_ln") as r_ln,
        nc.semaphore("r_table") as r_table,
        nc.semaphore("r_pool") as r_pool,
        nc.Block() as block,
    ):
        @block.scalar
        def _(act):
            act.preload_act_table_set(ACT_SET)
            rsqrt_table(act, Steps(act, r_ln, 1), rall[:, :, :], tmp[:, :, :], stats[:, :, :]).then_inc(r_table, 1)

        @block.gpsimd
        def _(pool):
            pool.memset(three[:, :, :], 3.0)
            pool.wait_ge(r_table, 1)
            rsqrt_newton(pool, Steps(pool, r_pool, 3), rall[:, :, :], stats[:, :, :], tmp[:, :, :], three[:, :, :])


def layer(nc, d, out):
    mixed = nc.dram_tensor("mixed", (TILES, P, D), F32, kind="Internal").ap()
    with (
        nc.sbuf_tensor("group_stats", [P, TILES, 3], F32) as stats,
        nc.sbuf_tensor("group_rstds", [P, TILES, 3], F32) as rall,
        nc.sbuf_tensor("group_tmp", [P, TILES, 3], F32) as tmp,
        nc.sbuf_tensor("group_three", [P, TILES, 3], F32) as three,
    ):
        mixer_phase(nc, d["x"], d["mem"], d["cols"], d["gain_mix"], d["gain_mem"], d["masks"], d["ident"],
                    d["w_in"], d["w_mem"], mixed, stats)
        group_rstds(nc, stats, rall, tmp, three)
        for half in range(2):
            with (
                nc.sbuf_tensor(f"y_{half}", [P, HT, D], F32) as y,
                nc.sbuf_tensor(f"y_high_{half}", [P, DC, HALF], F32R) as xh,
                nc.sbuf_tensor(f"y_low_{half}", [P, DC, HALF], F32R) as xl,
            ):
                out_phase(nc, half, d["x"], mixed, d["w_out"], d["out_gain"], d["gain_ffn"], d["ident"], rall, y, xh, xl)
                ffn_phase(nc, half, d["w_gu"], d["w_down"], out, y, xh, xl)


def lay_out(i):
    def rows(a, *shape):
        return np.ascontiguousarray(a, dtype=a.dtype).reshape(shape)

    def by_partition(w):
        return np.ascontiguousarray(w.reshape(-1, P, w.shape[-1]).transpose(1, 0, 2))

    w_in = i["w_in"][0]
    heads = [h for j in range(4) for h in (j, 4 + j)]
    q = w_in[:, :512].reshape(D, HEADS, HD)[:, heads].reshape(D, 512)
    k, v = w_in[:, 512:640], w_in[:, 640:768]
    h, b, c, mq = (w_in[:, 768 + 256 * n:1024 + 256 * n] for n in range(4))
    cols = np.zeros((P, COLS), np.float32)
    for at, name in ((QG, "q_norm"), (KG, "k_norm"), (MQG, "mem_q_norm"), (MKG, "mem_k_norm")):
        cols[:, at] = np.concatenate([i[name][0]] * 2)
    for ch in range(CC):
        cols[:, CW + 3 * ch:CW + 3 * ch + 3] = i["conv_w"][0][:, ch * P:(ch + 1) * P].T
        cols[:, CB + ch] = i["conv_b"][0][ch * P:(ch + 1) * P]
    cols[:, SINK:SINK + HEADS] = i["attn_sinks"][0][None, :]
    cols[:, MEANS:MEANS + 3] = [4 / 512, 4 / 256, 4 / 256]
    cols[:, EPS4] = 4 * EPS
    cols[:, THREE] = 3.0
    cols[:, ONE] = 1.0
    dist = (np.arange(P)[:, None] + P - np.arange(KEYS)[None, :])
    slopes = (2.0 ** (-8.0 * np.arange(1, HEADS + 1) / HEADS)).astype(np.float32)
    bias = -slopes[None, :, None] * dist[:, None, :].astype(np.float32)
    masks = np.where(((dist >= 0) & (dist < P))[:, None, :], bias, np.float32(MASKED)).astype(np.float32)
    order = np.concatenate([np.arange(h * HD, h * HD + HD) for h in heads] + [np.arange(512, 1024)])
    w_out = i["w_out"][0][order]
    out_gain = np.concatenate([i["out_norm_attn"][0], i["out_norm_conv"][0], i["out_norm_mem"][0]])[order]
    gate, up = (i[n][0].reshape(DC, P, 2 * PAIRS, P) for n in ("w_gate", "w_up"))
    w_gu = np.stack([gate, up]).transpose(3, 2, 0, 1, 4)
    w_down = i["w_down"][0].reshape(PAIRS, 2, P, D).transpose(0, 2, 1, 3)
    return {
        "x": rows(i["x"], TILES, P, D),
        "mem": rows(i["mem"], 2, P, D),
        "cols": cols,
        "gain_mix": np.repeat(i["norm_mix"], P, axis=0),
        "gain_mem": np.repeat(i["norm_mem"], P, axis=0),
        "gain_ffn": np.repeat(i["norm_ffn"], P, axis=0),
        "masks": masks,
        "ident": np.eye(P, dtype=np.float32),
        "w_in": by_partition(np.concatenate([q, k, mq, v, h, c, b], axis=1)),
        "w_mem": by_partition(i["w_mem_kv"][0]).reshape(P, -1),
        "w_out": by_partition(w_out),
        "out_gain": np.ascontiguousarray(out_gain.reshape(DC, P).T),
        "w_gu": np.ascontiguousarray(w_gu).reshape(2 * PAIRS, P, 2 * DC * P),
        "w_down": np.ascontiguousarray(w_down).reshape(PAIRS, P, 2 * D),
    }


def kernel(**inputs):
    from concourse import bacc
    from concourse.bass_utils import run_bass_kernel_spmd

    nc = bacc.Bacc("TRN2", target_bir_lowering=False, num_devices=1)
    arrays = {f"in_{n}": a for n, a in lay_out({n: np.asarray(a) for n, a in inputs.items()}).items()}
    aps = {n[3:]: nc.dram_tensor(n, a.shape, F32, kind="ExternalInput").ap() for n, a in arrays.items()}
    out = nc.dram_tensor("out", (TILES, P, D), F32, kind="ExternalOutput").ap()
    layer(nc, aps, out)
    return run_bass_kernel_spmd(nc, [arrays], core_ids=[0]).results[0]["out"].reshape(1, SEQ, D)
```

```python
from contextlib import ExitStack

import numpy as np

import concourse.bass as bass
from concourse import mybir

F32 = mybir.dt.float32
F32R = mybir.dt.float32r
ALU = mybir.AluOpType
ACT = mybir.ActivationFunctionType
AX_X = mybir.AxisListType.X

P = 128
D = 1024
DC = D // P
SEQ = 2048
TILES = SEQ // P
HD = 64
HEADS = 8
CONV_CH = 256
CC = CONV_CH // P
MEM = 256
MEM_HEADS = 4
MEM_W = MEM_HEADS * HD
UNITS = 6
SLOTS = 2 * UNITS
KEYS = 2 * P
QK = 512 + P + MEM_W
QK_HEADS = QK // HD
PROJ = 2 * QK
GROUP = 448
GROUPS = PROJ // GROUP
FF = 2816
PAIRS = FF // (2 * P)
HALF = SEQ // 2
HT = HALF // P
BANK = 512
EPS = 1e-6
MASKED = -1e30
ACT_SET = "natural_log_exp_and_others"

V0, H0, C0, B0 = 0, P, P + CONV_CH, P + 2 * CONV_CH
QG, KG, MQG, MKG, CW, CB, SINK, MEANS, EPS4, THREE, ONE, GAIN, COLS = 0, 1, 2, 3, 4, 10, 12, 20, 23, 24, 25, 26, 34
GROUP_CHUNKS = (range(0, 4), range(4, 6), range(6, 8))


def unit_heads(u):
    return 4 * (u % 2) + 2 * (u // 2) if u < 4 else 8 + 2 * (u - 4)


def unit_rows(u):
    e = u % 2
    return slice(HD * e, HD * e + HD)


class Parts:
    pass


class Steps:

    def __init__(self, engine, semaphore, per):
        self.engine, self.semaphore, self.per, self.round, self.k = engine, semaphore, per, 0, 0

    def start(self, i):
        self.round, self.k = i, 0

    def then_wait(self, instruction):
        self.k += 1
        assert self.k <= self.per
        instruction.then_inc(self.semaphore, 1)
        self.engine.wait_ge(self.semaphore, self.round * self.per + self.k)


def three_passes(pe, out, wh, wl, xh, xl, start, stop):
    pe.matmul(out, wh, xh, start=start, stop=False)
    pe.matmul(out, wh, xl, start=False, stop=False)
    return pe.matmul(out, wl, xh, start=False, stop=stop)


def rsqrt_table(act, steps, z, ln, v4):
    steps.then_wait(act.activation(ln, v4, ACT.Ln))
    return act.activation(z, ln, ACT.Exp, scale=-0.5)


def rsqrt_newton(pool, steps, z, v4, t, three):
    steps.then_wait(pool.tensor_tensor(t, z, z, ALU.mult))
    steps.then_wait(pool.tensor_tensor(t, t, v4, ALU.mult))
    steps.then_wait(pool.tensor_tensor(t, three, t, ALU.subtract))
    return pool.tensor_tensor(z, z, t, ALU.mult)


def load_w_out(sp, o, c):
    if c >= 4:
        sp.wait_ge(o.wl_ready, c - 3)
    sp.dma_start(o.stage[c % 4], o.w_out[:, c, :]).then_inc(o.stage_in[c % 4], 16)


def high_w_out(act, o, c):
    act.wait_ge(o.stage_in[c % 4], 16 * (c // 4 + 1))
    act.activation(o.wh[:, c, :], o.stage[c % 4], ACT.Copy, scale=o.gains[:, c:c + 1]).then_inc(o.wh_ready, 1)


def low_w_out(dve, o, c):
    dve.wait_ge(o.wh_ready, c + 1)
    dve.scalar_tensor_tensor(out=o.wl[:, c, :], in0=o.stage[c % 4], scalar=o.gains[:, c:c + 1], in1=o.wh[:, c, :],
                             op0=ALU.mult, op1=ALU.subtract).then_inc(o.wl_ready, 1)


def load_mixed(sp, o, j):
    sp.dma_start(o.mt, o.mixed[j + o.first_tile]).then_inc(o.mt_in, 16)


def load_y(sp, o, part):
    tiles = slice(o.first_tile + 2 * part, o.first_tile + 2 * part + 2)
    sp.dma_start(o.y[:, 2 * part:2 * part + 2, :], o.x[tiles].rearrange("t p d -> p t d")).then_inc(o.y_in[part], 16)


def high_mixed(act, o, j):
    act.wait_ge(o.mt_in, 16 * j + 16)
    act.activation(o.mh[j % 2][:, :, :], o.mt, ACT.Copy).then_inc(o.mh_ready, 1)


def low_mixed(pool, o, j):
    pool.wait_ge(o.mh_ready, j + 1)
    pool.tensor_tensor(o.ml[j % 2][:, :, :], o.mt.rearrange("p (c q) -> p c q", c=DC), o.mh[j % 2][:, :, :],
                       ALU.subtract).then_inc(o.ml_ready, 1)


def out_group(pe, o, parts, slot, n, g, split=DC):
    for c in GROUP_CHUNKS[g]:
        if c >= split:
            pe.wait_ge(o.wl_ready, c + 1)
        done = three_passes(pe, parts[n][g][:, :], o.mh[slot][:, c, :], o.ml[slot][:, c, :],
                            o.wh[:, c, n * BANK:(n + 1) * BANK], o.wl[:, c, n * BANK:(n + 1) * BANK],
                            c == GROUP_CHUNKS[g][0], c == GROUP_CHUNKS[g][-1])
    return done


def group_table(act, o, shared):
    tiles = slice(o.first_tile, o.first_tile + HT)
    steps = Steps(act, shared.r_ln, 1)
    steps.start(o.half)
    rsqrt_table(act, steps, shared.rall[:, tiles, :], shared.tmp[:, tiles, :],
                shared.stats[:, tiles, :]).then_inc(shared.r_table, 1)


def group_newton(pool, o, shared):
    tiles = slice(o.first_tile, o.first_tile + HT)
    pool.wait_ge(shared.r_table, o.half + 1)
    steps = Steps(pool, shared.r_pool, 3)
    steps.start(o.half)
    rsqrt_newton(pool, steps, shared.rall[:, tiles, :], shared.stats[:, tiles, :],
                 shared.tmp[:, tiles, :], shared.three[:, tiles, :]).then_inc(shared.r_ready, 1)


def mixer_phase(nc, block, sem, banks, d, mixed, shared, o):
    x, x_turned_d, mem, cols, gain_mem, masks = d["x"], d["x_turned"], d["mem"], d["cols"], d["gain_mem"], d["masks"]
    w_in, w_mem, ident_d = d["w_in"], d["w_mem"], d["ident"]
    gain, ident, stats = shared.gain, shared.ident, shared.stats
    place = ExitStack()

    def sb(name, shape, dt=F32):
        return place.enter_context(nc.sbuf_tensor(name, shape, dt))

    wh = sb("w_in_high", [P, DC, PROJ], F32R)
    wl = sb("w_in_low", [P, DC, PROJ], F32R)
    xt = sb("xt", [P, D])
    xs = sb("xs", [P, D])
    with nc.sbuf_tensor("early_tiles", [P, 2, D], F32) as early_tiles:
        pass
    xh = sb("x_high", [P, DC, P], F32R)
    xl = sb("x_low", [P, DC, P], F32R)
    pq = sb("proj_qk", [P, QK])
    pv = sb("proj_vhcb", [P, QK])
    cy = sb("conv_sum", [P, CC, P])
    small = sb("small", [P, COLS])
    q8 = sb("q_gains_scaled", [P, 2])
    neg_sink = sb("neg_sink", [P, HEADS])
    mask = sb("mask", [P, HEADS, KEYS])
    v2 = sb("v_prev_cur", [P, 2, P])
    qT = sb("qT", [P, 4, P])
    mqT = sb("mem_qT", [P, 2, P])
    kT = sb("kT_prev_cur", [P, KEYS])
    uT = sb("uT", [P, CC, P + 2])
    bT = sb("bT", [P, CC, P])
    scores = sb("scores", [P, HEADS, KEYS + 1])
    region = sb("region", [P, SLOTS * (KEYS + 1) + 2 * HEADS * P])
    probs = region[:, 0:SLOTS * (KEYS + 1)].rearrange("p (h k) -> p h k", k=KEYS + 1)
    pT = region[:, SLOTS * (KEYS + 1):].rearrange("p (b h q) -> p b h q", b=2, h=HEADS)
    w_mem_sb = region[:, 0:DC * 2 * MEM_W].rearrange("p (c n) -> p c n", c=DC)
    memT = region[:, DC * 2 * MEM_W:DC * 2 * MEM_W + D].rearrange("p (c n) -> p c n", c=DC)
    region2 = sb("region2", [P, 2 * D + PROJ])
    mpT = region2[:, 0:D].rearrange("p (b h q) -> p b h q", b=2, h=MEM_HEADS)
    mix = region2[:, D:2 * D].rearrange("p (c q) -> p c q", c=DC)
    squares = region2[:, 2 * D:3 * D]
    sqmix = squares.rearrange("p (c q) -> p c q", c=DC)
    stage = [region2[:, 0:PROJ], region2[:, 2 * D:2 * D + PROJ],
             scores[:, :, :].rearrange("p h k -> p (h k)")[:, 0:PROJ],
             mask[:, :, :].rearrange("p h k -> p (h k)")[:, 0:PROJ]]
    early = [xt[:, :], early_tiles[:, 0, :], early_tiles[:, 1, :]]
    km = [pq[:, 0:MEM_W], pv[:, 0:MEM_W]]
    km_sq = sb("mem_k_squares", [P, MEM_W])
    kmT = sb("mem_kT", [P, 2, MEM])
    vm = sb("mem_v", [P, 2, MEM_W])
    ssq = sb("ssq", [P, 1])
    xv = sb("x_var", [P, 1])
    xln = sb("x_ln", [P, 1])
    xr = sb("x_rstd", [P, 1])
    xn2 = sb("x_newton", [P, 1])
    qss = sb("qk_ss", [P, QK_HEADS])
    qv = sb("qk_var", [P, QK_HEADS])
    qln = sb("qk_ln", [P, QK_HEADS])
    qr = sb("qk_rstd", [P, QK_HEADS])
    qn2 = sb("qk_newton", [P, QK_HEADS])
    mx = sb("row_max", [P, SLOTS])
    nm = sb("neg_max", [P, SLOTS])
    rs = sb("row_sum", [P, SLOTS])
    rr = sb("row_rcp", [P, SLOTS])

    place.close()

    turn, proj, sc, att = banks[0:2], banks[2:4], banks[4:6], banks[6]
    matt = banks[7]
    first_proj = banks[2:6]

    final_steps = Parts()
    small_in = sem("small_in")
    mask_in = sem("mask_in")
    gain_mem_in = sem("gain_mem_in")
    w_mem_in = sem("w_mem_in")
    early_in = [sem("mem0_in"), sem("mem1_in"), sem("x0_in")]
    x_in = sem("x_in")
    xT_in = sem("xT_in")
    stage_in = [sem(f"stage{j}_in") for j in range(4)]
    mix_out = sem("mix_out")
    prepared = sem("prepared")
    sinks_set = sem("sinks_set")
    cleared = sem("cleared")
    wh_ready = sem("wh_ready")
    wl_ready = sem("wl_ready")
    xy_ready = sem("xy_ready")
    xr_ready = sem("xr_ready")
    xs_ready = sem("xs_ready")
    x_turned = sem("x_turned")
    xh_ready = sem("xh_ready")
    xl_ready = sem("xl_ready")
    memT_ready = sem("memT_ready")
    kv_done = sem("kv_done")
    kv_taken = sem("kv_taken")
    q_squared = sem("q_squared")
    qss_ready = sem("qss_ready")
    qy_ready = sem("qy_ready")
    qn_ready = sem("qn_ready")
    km_turned = sem("km_turned")
    km_ready = sem("km_ready")
    proj_done = sem("proj_done")
    proj_taken = sem("proj_taken")
    q_turned = sem("q_turned")
    qT_ready = sem("qT_ready")
    k_shifted = sem("k_shifted")
    v_shifted = sem("v_shifted")
    u_ready = sem("u_ready")
    hist_ready = sem("hist_ready")
    conv_turned = sem("conv_turned")
    convT_ready = sem("convT_ready")
    scores_done = sem("scores_done")
    max_ready = sem("max_ready")
    exp_ready = sem("exp_ready")
    probs_ready = sem("probs_ready")
    p_turned = sem("p_turned")
    pT_ready = sem("pT_ready")
    pv_done = sem("pv_done")
    mpv_done = sem("mpv_done")
    mix_parts = sem("mix_parts")
    mix_squared = sem("mix_squared")
    stats_done = sem("stats_done")
    stats_taken = sem("stats_taken")
    act_x, act_q = sem("act_x"), sem("act_q")
    pool_x, pool_q, pool_v, pool_s = sem("pool_x"), sem("pool_q"), sem("pool_v"), sem("pool_s")
    dve_max, dve_sum, dve_conv = sem("dve_max"), sem("dve_sum"), sem("dve_conv")

    @block.sync
    def _(sp):
        def load_xT(t):
            sp.dma_start(xs[:, :], x_turned_d[t]).then_inc(xT_in, 16)

        sp.dma_start(early[0], mem[0]).then_inc(early_in[0], 16)
        sp.dma_start(gain[:, :], gain_mem).then_inc(gain_mem_in, 16)
        sp.dma_start(region[:, 0:DC * 2 * MEM_W], w_mem).then_inc(w_mem_in, 16)
        for c in range(4):
            sp.dma_start(stage[c], w_in[:, c, :]).then_inc(stage_in[c], 16)
        sp.wait_ge(x_turned, 4)
        load_xT(0)
        for c in range(4, DC):
            sp.wait_ge(wl_ready, c - 3)
            sp.dma_start(stage[c % 4], w_in[:, c, :]).then_inc(stage_in[c % 4], 16)
        sp.dma_start(xt[:, :], x[1]).then_inc(x_in, 16)
        sp.wait_ge(xl_ready, 1)
        load_xT(1)
        sp.wait_ge(wl_ready, DC)
        sp.dma_start(mask[:, :, :], masks).then_inc(mask_in, 16)
        sp.dma_start(shared.out_gains[:, :], d["out_gain"]).then_inc(shared.out_gains_in, 16)
        sp.dma_start(gain[:, :], d["gain_ffn"]).then_inc(shared.gain_ffn_in, 16)

        def store(t):
            sp.wait_ge(mix_parts, 3 * t + 3)
            sp.dma_start(mixed[t], region2[:, D:2 * D]).then_inc(mix_out, 16)

        with sp.Fori(0, TILES - 2) as t:
            sp.wait_ge(xl_ready, t + 2)
            load_xT(t + 2)
            sp.wait_ge(xy_ready, t + 4)
            sp.dma_start(xt[:, :], x[t + 2]).then_inc(x_in, 16)
            store(t)
        store(TILES - 2)
        sp.wait_ge(proj_done, GROUPS * TILES)
        sp.wait_ge(mix_out, 16 * HT)
        load_mixed(sp, o, 0)
        for c in range(DC):
            load_w_out(sp, o, c)
        sp.wait_ge(o.ml_ready, 1)
        load_mixed(sp, o, 1)
        for part in range(2):
            load_y(sp, o, part)
        store(TILES - 1)
        sp.wait_ge(o.ml_ready, 2)
        load_mixed(sp, o, 2)
        for part in range(2, 4):
            load_y(sp, o, part)

    @block.tensor
    def _(pe):
        def turn_x(i):
            pe.wait_ge(xs_ready, i + 1)
            for b in range(2):
                for c in range(4):
                    last = pe.transpose(turn[b][:, c * P:(c + 1) * P], xs[:, (4 * b + c) * P:(4 * b + c + 1) * P],
                                        ident[:, :])
                last.then_inc(x_turned, 1)

        def project_chunk(bank, g, c):
            cols_g = slice(g * GROUP, (g + 1) * GROUP)
            return three_passes(pe, bank[:, 0:GROUP], xh[:, c, :], xl[:, c, :],
                                wh[:, c, cols_g], wl[:, c, cols_g], c == 0, c == DC - 1)

        def project(g):
            for c in range(DC):
                last = project_chunk(proj[g % 2], g, c)
            last.then_inc(proj_done, 1)

        def scores_of(*units):
            for n in range(2):
                for u in units:
                    rows = unit_rows(u)
                    if u < 4:
                        q, keys = qT[rows, 2 * (u // 2) + n, :], kT[rows, :]
                    else:
                        q, keys = mqT[rows, n, :], kmT[rows, n, :]
                    done = pe.matmul(sc[u % 2][:, n * KEYS:(n + 1) * KEYS], q, keys, start=True, stop=True)
                    if n == 1:
                        done.then_inc(scores_done, 1)

        def turn_probs(t, u):
            pe.wait_ge(probs_ready, UNITS * t + u + 1)
            to = turn[(u + 1) % 2]
            for b in range(2):
                for n in range(2):
                    last = pe.transpose(to[:, (2 * b + n) * P:(2 * b + n + 1) * P],
                                        probs[:, unit_heads(u) + n, b * P:(b + 1) * P], ident[:, :])
            last.then_inc(p_turned, 1)

        def turn_qk(t):
            pe.wait_ge(qn_ready, t + 3)
            for c in range(4):
                last = pe.transpose(turn[1][:, c * P:(c + 1) * P], pq[:, c * P:(c + 1) * P], ident[:, :])
            last.then_inc(q_turned, 1)
            for c in range(3):
                last = pe.transpose(turn[0][:, c * P:(c + 1) * P], pq[:, (4 + c) * P:(5 + c) * P], ident[:, :])
            last.then_inc(q_turned, 1)

        def turn_conv():
            for j, col in enumerate((C0, C0 + P, B0, B0 + P)):
                last = pe.transpose(turn[0][:, j * P:(j + 1) * P], pv[:, col:col + P], ident[:, :])
            last.then_inc(conv_turned, 1)

        def mean_squares(t, bank=matt):
            pe.wait_ge(mix_squared, t + 1)
            for j, chunks in enumerate(GROUP_CHUNKS):
                last = pe.matmul(bank[:, j:j + 1], sqmix[:, chunks[0], :], small[:, MEANS + j:MEANS + j + 1],
                                 start=True, stop=True)
            last.then_inc(stats_done, 1)

        def window_attention():
            for b in range(2):
                for g in range(2):
                    rows = slice(HD * g, HD * g + HD)
                    done = pe.matmul(att[rows, :], v2[:, b, rows], pT[:, b, 4 * g:4 * g + 4, :],
                                     start=(b == 0), stop=(b == 1))
            done.then_inc(pv_done, 1)

        def memory_attention():
            for c in range(2):
                for b in range(2):
                    for e in range(2):
                        rows = slice(HD * e, HD * e + HD)
                        head = slice(HD * (2 * c + e), HD * (2 * c + e) + HD)
                        done = pe.matmul(matt[rows, c * P:(c + 1) * P], vm[:, b, head], mpT[:, b, 2 * e + c, :],
                                         start=(b == 0), stop=(b == 1))
            done.then_inc(mpv_done, 1)

        def tile(t, first=False, final=False):
            nxt = t + 1

            def project_next(g):
                if not final:
                    pe.wait_ge(proj_taken, GROUPS * nxt + g - 1)
                    project(g)

            pe.wait_ge(qT_ready, 3 * t + 3)
            if not first:
                pe.wait_ge(exp_ready, UNITS * t)
            scores_of(0, 1)
            pe.wait_ge(u_ready, t + 1)
            turn_conv()
            if not final:
                pe.wait_ge(xl_ready, nxt + 1)
            project_next(0)
            pe.wait_ge(max_ready, UNITS * t + 1)
            scores_of(2)
            turn_probs(t, 0)
            if not first:
                mean_squares(t - 1)
            project_next(1)
            pe.wait_ge(max_ready, UNITS * t + 3)
            scores_of(3, 4)
            pe.wait_ge(convT_ready, t + 1)
            turn_probs(t, 1)
            pe.wait_ge(pT_ready, UNITS * t + 1)
            turn_probs(t, 2)
            project_next(2)
            pe.wait_ge(max_ready, UNITS * t + 4)
            scores_of(5)
            pe.wait_ge(pT_ready, UNITS * t + 2)
            turn_probs(t, 3)
            project_next(3)
            if final:
                pe.wait_ge(o.ml_ready, 1)
                pe.wait_ge(proj_taken, GROUPS * TILES)
                out_group(pe, o, [proj[0:1], proj[1:2]], 0, 0, 0, split=0)
            pe.wait_ge(pT_ready, UNITS * t + 3)
            turn_probs(t, 4)
            pe.wait_ge(pT_ready, UNITS * t + 4)
            turn_probs(t, 5)
            if final:
                out_group(pe, o, [proj[0:1], proj[1:2]], 0, 1, 0)
            pe.wait_ge(v_shifted, t + 1)
            if not first:
                pe.wait_ge(mix_parts, 3 * t)
            window_attention()
            pe.wait_ge(pT_ready, UNITS * t + 6)
            if not final:
                turn_qk(nxt)
            if not first:
                pe.wait_ge(stats_taken, t)
            memory_attention()

        pe.wait_ge(small_in, 32)
        def turn_km(m):
            pe.wait_ge(qn_ready, m + 1)
            for c in range(2):
                last = pe.transpose(turn[0][:, c * P:(c + 1) * P], km[m][:, c * P:(c + 1) * P], ident[:, :])
            last.then_inc(km_turned, 1)

        for m in range(2):
            turn_x(m)
            if m == 0:
                pe.wait_ge(w_mem_in, 16)
            pe.wait_ge(memT_ready, m + 1)
            for c in range(DC):
                last = pe.matmul(proj[m][:, :], memT[:, c, :], w_mem_sb[:, c, :], start=(c == 0), stop=(c == DC - 1))
            last.then_inc(kv_done, 1)
        pe.wait_ge(xl_ready, 1)
        pe.wait_ge(kv_taken, 2)
        for c in range(DC):
            pe.wait_ge(wl_ready, c + 1)
            for g in range(GROUPS if c < DC // 2 else 2):
                done = project_chunk(first_proj[g], g, c)
                if c == DC - 1:
                    done.then_inc(proj_done, 1)
            if c == 1:
                turn_km(0)
            if c == 4:
                pe.wait_ge(km_ready, 1)
                turn_km(1)
        for g in range(2, GROUPS):
            for c in range(DC // 2, DC):
                done = project_chunk(first_proj[g], g, c)
            done.then_inc(proj_done, 1)
        pe.wait_ge(km_ready, 2)
        turn_qk(0)
        tile(0, first=True)
        with pe.Fori(1, TILES - 1) as t:
            tile(t)
        tile(TILES - 1, final=True)
        final_steps.mean_squares = lambda: mean_squares(TILES - 1, turn[1])

    @block.scalar
    def _(act):
        x_steps = Steps(act, act_x, 3)
        q_steps = Steps(act, act_q, 2)

        def x_rstd(i, early_tile=None):
            tile = xt[:, :]
            if early_tile is not None:
                tile = early_tile
                act.wait_ge(early_in[i], 16)
            else:
                act.wait_ge(x_in, 16 * i - 32)
                act.wait_ge(proj_taken, GROUPS * (i - 2))
            x_steps.start(i)
            if early_tile is not None and i < 2:
                if i:
                    act.wait_ge(x_turned, 2 * i)
                squares_to = xs[:, :]
            else:
                squares_to = tile
            x_steps.then_wait(act.activation(squares_to, tile, ACT.Square, accum_out=ssq[:, :]))
            x_steps.then_wait(act.activation(xv[:, :], ssq[:, :], ACT.Identity, bias=small[:, EPS4:EPS4 + 1],
                                             scale=4.0 / D))
            rsqrt_table(act, x_steps, xr[:, :], xln[:, :], xv[:, :]).then_inc(xy_ready, 1)

        def q_rstd(i, n=QK_HEADS):
            act.wait_ge(qss_ready, i + 1)
            q_steps.start(i)
            q_steps.then_wait(act.activation(qv[:, 0:n], qss[:, 0:n], ACT.Identity, bias=small[:, EPS4:EPS4 + 1],
                                             scale=4.0 / HD))
            rsqrt_table(act, q_steps, qr[:, 0:n], qln[:, 0:n], qv[:, 0:n]).then_inc(qy_ready, 1)

        def split_x(t, first=False):
            act.wait_ge(xT_in, 16 * t + 16)
            if not first:
                act.wait_ge(proj_done, GROUPS * t)
            act.activation(xh[:, :, :], xs[:, :], ACT.Copy).then_inc(xh_ready, 1)

        def take_proj(t, g, first=False):
            act.wait_ge(proj_done, GROUPS * t + g + 1)
            if g == 0:
                act.wait_ge(xr_ready, t + 3)
            if g == 2 and not first:
                act.wait_ge(v_shifted, t)
            to = pq if g < 2 else pv
            bank = first_proj[g] if first else proj[g % 2]
            act.activation(to[:, (g % 2) * GROUP:(g % 2 + 1) * GROUP], bank[:, 0:GROUP],
                           ACT.Copy, scale=xr[:, 0:1]).then_inc(proj_taken, 1)

        def take_qT(t):
            act.wait_ge(q_turned, 2 * t + 1)
            act.activation(qT[:, :, :], turn[1][:, :], ACT.Copy, scale=q8[:, 0:1]).then_inc(qT_ready, 1)
            act.wait_ge(q_turned, 2 * t + 2)
            act.wait_ge(k_shifted, t + 1)
            act.activation(kT[:, P:KEYS], turn[0][:, 0:P], ACT.Copy, scale=small[:, KG:KG + 1]).then_inc(qT_ready, 1)
            act.activation(mqT[:, :, :], turn[0][:, P:3 * P], ACT.Copy, scale=q8[:, 1:2]).then_inc(qT_ready, 1)

        def take_convT(t):
            act.wait_ge(conv_turned, t + 1)
            act.wait_ge(hist_ready, t + 1)
            act.activation(uT[:, :, 2:P + 2], turn[0][:, 0:CONV_CH].rearrange("p (c q) -> p c q", c=CC), ACT.Copy)
            act.activation(bT[:, :, :], turn[0][:, CONV_CH:2 * CONV_CH].rearrange("p (c q) -> p c q", c=CC),
                           ACT.Copy).then_inc(convT_ready, 1)

        def exps(t, u, first=False):
            act.wait_ge(max_ready, UNITS * t + u + 1)
            if first:
                act.wait_ge(cleared, 1)
                act.wait_ge(sinks_set, 1)
            else:
                act.wait_ge(p_turned, UNITS * (t - 1) + u + 1)
            lo = P if first else 0
            for n in range(2):
                h = unit_heads(u) + n
                if u < 4:
                    out, of = probs[:, h, lo:KEYS + 1], scores[:, h, lo:KEYS + 1]
                else:
                    out, of = probs[:, h, 0:KEYS], sc[u % 2][:, n * KEYS:(n + 1) * KEYS]
                last = act.activation(out, of, ACT.Exp, bias=nm[:, h:h + 1], accum_out=rs[:, h:h + 1])
            last.then_inc(exp_ready, 1)

        def take_pT(t, u, first=False):
            act.wait_ge(p_turned, UNITS * t + u + 1)
            if not first:
                act.wait_ge(pv_done if u < 4 else mpv_done, t)
            h = unit_heads(u)
            to = pT[:, :, h:h + 2, :] if u < 4 else mpT[:, :, h - 8:h - 6, :]
            act.activation(to, turn[(u + 1) % 2][:, :].rearrange("p (b h q) -> p b h q", b=2, h=2),
                           ACT.Copy).then_inc(pT_ready, 1)

        def split_w(c):
            act.wait_ge(stage_in[c % 4], 16 * (c // 4 + 1))
            act.activation(wh[:, c, :], stage[c % 4], ACT.Copy, scale=small[:, GAIN + c:GAIN + c + 1]).then_inc(wh_ready, 1)

        def tile(t, first=False, final=False):
            nxt = t + 1
            if not (first or final):
                split_x(nxt)
                x_rstd(nxt + 2)
            exps(t, 0, first)
            exps(t, 1, first)
            take_convT(t)
            if final:
                act.wait_ge(shared.out_gains_in, 16)
                high_mixed(act, o, 0)
                high_w_out(act, o, 0)
                high_w_out(act, o, 1)
            else:
                take_proj(nxt, 0)
            exps(t, 2, first)
            take_pT(t, 0, first)
            if final:
                high_w_out(act, o, 2)
                high_w_out(act, o, 3)
            else:
                take_proj(nxt, 1)
            exps(t, 3, first)
            take_pT(t, 1, first)
            exps(t, 4, first)
            take_pT(t, 2, first)
            if final:
                high_w_out(act, o, 4)
            else:
                take_proj(nxt, 2)
                q_rstd(nxt + 2)
            exps(t, 5, first)
            take_pT(t, 3, first)
            if final:
                high_w_out(act, o, 5)
                act.wait_ge(stats_taken, HT)
                group_table(act, o, shared)
            else:
                take_proj(nxt, 3)
            take_pT(t, 4, first)
            take_pT(t, 5, first)
            if final:
                high_w_out(act, o, 6)
                high_w_out(act, o, 7)
            else:
                take_qT(nxt)

        def take_memT(m):
            for b in range(2):
                act.wait_ge(x_turned, 2 * m + b + 1)
                last = act.activation(memT[:, 4 * b:4 * b + 4, :], turn[b][:, :], ACT.Copy)
            last.then_inc(memT_ready, 1)

        def take_kv(m):
            act.wait_ge(kv_done, m + 1)
            act.activation(km[m], proj[m][:, 0:MEM_W], ACT.Copy)
            act.activation(vm[:, m, :], proj[m][:, MEM_W:2 * MEM_W], ACT.Copy).then_inc(kv_taken, 1)

        def take_kmT(m):
            act.wait_ge(km_turned, m + 1)
            act.activation(kmT[:, :, m * P:(m + 1) * P], turn[0][:, 0:2 * P].rearrange("p (c q) -> p c q", c=2),
                           ACT.Copy, scale=small[:, MKG:MKG + 1]).then_inc(km_ready, 1)

        act.dma_start(small[:, :], cols).then_inc(small_in, 16)
        act.dma_start(ident[:, :], ident_d).then_inc(small_in, 16)
        act.dma_start(early[1], mem[1]).then_inc(early_in[1], 16)
        act.dma_start(early[2], x[0]).then_inc(early_in[2], 16)
        act.preload_act_table_set(ACT_SET)
        act.wait_ge(small_in, 32)
        x_rstd(0, early[0])
        take_memT(0)
        x_rstd(1, early[1])
        split_w(0)
        take_memT(1)
        x_rstd(2, early[2])
        take_kv(0)
        split_w(1)
        split_x(0, first=True)
        split_w(2)
        take_kv(1)
        q_rstd(0, MEM_HEADS)
        split_w(3)
        split_w(4)
        take_kmT(0)
        q_rstd(1, MEM_HEADS)
        for c in range(5, DC):
            split_w(c)
        take_kmT(1)
        for g in range(GROUPS):
            take_proj(0, g, first=True)
            if g == 2:
                q_rstd(2)
        split_x(1)
        x_rstd(3)
        act.wait_ge(prepared, 1)
        take_qT(0)
        tile(0, first=True)
        with act.Fori(1, TILES - 2) as t:
            tile(t)
        tile(TILES - 2)
        tile(TILES - 1, final=True)

    @block.vector
    def _(dve):
        max_steps = Steps(dve, dve_max, 2 * 4 + 2)
        sum_steps = Steps(dve, dve_sum, UNITS)
        conv_steps = Steps(dve, dve_conv, 3)

        def scale_x(i, of):
            dve.wait_ge(xr_ready, i + 1)
            dve.scalar_tensor_tensor(out=xs[:, :], in0=of, scalar=xr[:, 0:1], in1=gain[:, :],
                                     op0=ALU.mult, op1=ALU.mult).then_inc(xs_ready, 1)

        def low_x(t):
            dve.wait_ge(xh_ready, t + 1)
            dve.tensor_tensor(xl[:, :, :], xs[:, :].rearrange("p (c q) -> p c q", c=DC), xh[:, :, :],
                              ALU.subtract).then_inc(xl_ready, 1)

        def low_w(c):
            dve.wait_ge(wh_ready, c + 1)
            dve.scalar_tensor_tensor(out=wl[:, c, :], in0=stage[c % 4], scalar=small[:, GAIN + c:GAIN + c + 1],
                                     in1=wh[:, c, :], op0=ALU.mult, op1=ALU.subtract).then_inc(wl_ready, 1)

        def head_sums(i, of, n=QK_HEADS):
            dve.wait_ge(q_squared, i + 1)
            dve.tensor_reduce(qss[:, 0:n], of.rearrange("p (h d) -> p h d", d=HD), AX_X, ALU.add).then_inc(qss_ready, 1)

        def maxima(t, u, first=False):
            if not first:
                dve.wait_ge(exp_ready, UNITS * (t - 1) + u + 1)
            dve.wait_ge(scores_done, UNITS * t + u + 1)
            h0 = unit_heads(u)
            if u < 4:
                lo = P if first else 0
                biased = scores[:, h0:h0 + 2, lo:KEYS]
                of = sc[u % 2][:, :].rearrange("p (n k) -> p n k", n=2)[:, :, lo:KEYS]
                max_steps.then_wait(dve.tensor_tensor(biased, of, mask[:, h0:h0 + 2, lo:KEYS], ALU.add))
                max_steps.then_wait(dve.tensor_reduce(mx[:, h0:h0 + 2], biased, AX_X, ALU.max))
                dve.scalar_tensor_tensor(out=nm[:, h0:h0 + 2], in0=mx[:, h0:h0 + 2], scalar=-1.0,
                                         in1=neg_sink[:, h0:h0 + 2], op0=ALU.mult, op1=ALU.min).then_inc(max_ready, 1)
            else:
                max_steps.then_wait(dve.tensor_reduce(mx[:, h0:h0 + 2], sc[u % 2][:, :].rearrange("p (n k) -> p n k", n=2),
                                                      AX_X, ALU.max))
                dve.tensor_scalar(nm[:, h0:h0 + 2], mx[:, h0:h0 + 2], -1.0, None, ALU.mult).then_inc(max_ready, 1)

        def divide(t, u):
            dve.wait_ge(exp_ready, UNITS * t + u + 1)
            h0 = unit_heads(u)
            sum_steps.then_wait(dve.reciprocal(rr[:, h0:h0 + 2], rs[:, h0:h0 + 2]))
            for h in (h0, h0 + 1):
                last = dve.tensor_scalar(probs[:, h, 0:KEYS], probs[:, h, 0:KEYS], rr[:, h:h + 1], None, ALU.mult)
            last.then_inc(probs_ready, 1)

        def convolve(t, first=False):
            dve.wait_ge(convT_ready, t + 1)
            if not first:
                dve.wait_ge(mix_out, 16 * t)
                dve.wait_ge(mix_squared, t)
            conv_steps.start(t)
            for c in range(CC):
                last = dve.tensor_scalar(cy[:, c, :], uT[:, c, 0:P], small[:, CW + 3 * c:CW + 3 * c + 1], None, ALU.mult)
            conv_steps.then_wait(last)
            for j in (1, 2):
                for c in range(CC):
                    w = small[:, CW + 3 * c + j:CW + 3 * c + j + 1]
                    last = dve.scalar_tensor_tensor(out=cy[:, c, :], in0=uT[:, c, j:j + P], scalar=w, in1=cy[:, c, :],
                                                    op0=ALU.mult, op1=ALU.add)
                conv_steps.then_wait(last)
            for c in range(CC):
                last = dve.scalar_tensor_tensor(out=mix[:, 4 + c, :], in0=cy[:, c, :], scalar=small[:, CB + c:CB + c + 1],
                                                in1=bT[:, c, :], op0=ALU.add, op1=ALU.mult)
            last.then_inc(mix_parts, 1)

        def take_attention(t):
            dve.wait_ge(pv_done, t + 1)
            dve.tensor_copy(region2[:, D:D + 4 * P], att[:, :]).then_inc(mix_parts, 1)
            dve.wait_ge(mpv_done, t + 1)
            dve.tensor_copy(region2[:, D + 6 * P:D + 8 * P], matt[:, 0:2 * P]).then_inc(mix_parts, 1)

        def take_stats(t, bank=matt):
            dve.wait_ge(stats_done, t + 1)
            dve.tensor_scalar(stats[:, t, :], bank[:, 0:3], 4 * EPS, None, ALU.add).then_inc(stats_taken, 1)

        def tile(t, first=False, final=False):
            nxt = t + 1
            max_steps.start(t)
            sum_steps.start(t)
            if not (first or final):
                low_x(nxt)
            maxima(t, 0, first)
            maxima(t, 1, first)
            divide(t, 0)
            if not first:
                take_stats(t - 1)
            maxima(t, 2, first)
            divide(t, 1)
            divide(t, 2)
            if final:
                dve.wait_ge(shared.out_gains_in, 16)
                low_w_out(dve, o, 0)
                low_w_out(dve, o, 1)
            maxima(t, 3, first)
            if not final:
                head_sums(nxt + 2, squares[:, 0:QK])
            maxima(t, 4, first)
            divide(t, 3)
            if final:
                low_w_out(dve, o, 2)
            maxima(t, 5, first)
            divide(t, 4)
            if final:
                low_w_out(dve, o, 3)
            convolve(t, first)
            divide(t, 5)
            if final:
                for c in range(4, DC):
                    low_w_out(dve, o, c)
            take_attention(t)

        dve.wait_ge(gain_mem_in, 16)
        dve.wait_ge(small_in, 32)
        scale_x(0, early[0])
        scale_x(1, early[1])
        low_w(0)
        low_w(1)
        low_x(0)
        low_w(2)
        head_sums(0, km_sq[:, :], MEM_HEADS)
        low_w(3)
        head_sums(1, km_sq[:, :], MEM_HEADS)
        for c in range(4, DC):
            low_w(c)
        head_sums(2, squares[:, 0:QK])
        low_x(1)
        dve.wait_ge(mask_in, 16)
        dve.wait_ge(prepared, 1)
        tile(0, first=True)
        with dve.Fori(1, TILES - 2) as t:
            tile(t)
        tile(TILES - 2)
        tile(TILES - 1, final=True)
        final_steps.take_stats = lambda: take_stats(TILES - 1, turn[1])

    @block.gpsimd
    def _(pool):
        x_steps = Steps(pool, pool_x, 3)
        q_steps = Steps(pool, pool_q, 4)
        v_steps = Steps(pool, pool_v, 1)
        s_steps = Steps(pool, pool_s, 2)

        def copy(to, of):
            one = small[:, ONE:ONE + 1]
            if len(of.shape) == 3:
                one = one.unsqueeze(2)
            return pool.tensor_tensor(to, of, one.to_broadcast(list(of.shape)), ALU.mult)

        def x_newton(i):
            pool.wait_ge(xy_ready, i + 1)
            x_steps.start(i)
            rsqrt_newton(pool, x_steps, xr[:, :], xv[:, :], xn2[:, :], small[:, THREE:THREE + 1]).then_inc(xr_ready, 1)

        def q_square(i, out, of):
            pool.tensor_tensor(out, of, of, ALU.mult).then_inc(q_squared, 1)

        def q_norm(i, of, n=QK_HEADS):
            pool.wait_ge(qy_ready, i + 1)
            q_steps.start(i)
            three = small[:, THREE:THREE + 1].to_broadcast([P, n])
            q_steps.then_wait(rsqrt_newton(pool, q_steps, qr[:, 0:n], qv[:, 0:n], qn2[:, 0:n], three))
            heads = of.rearrange("p (h d) -> p h d", d=HD)
            by = qr[:, 0:n].unsqueeze(2).to_broadcast([P, n, HD])
            pool.tensor_tensor(heads, heads, by, ALU.mult).then_inc(qn_ready, 1)

        def square_proj(t, wait_stats=True):
            pool.wait_ge(proj_taken, GROUPS * t + 2)
            if wait_stats:
                pool.wait_ge(stats_done, t - 1)
            q_square(t + 2, squares[:, 0:QK], pq[:, :])

        def shift_k(t):
            pool.wait_ge(scores_done, UNITS * (t - 1) + 4)
            copy(kT[:, 0:P], kT[:, P:KEYS]).then_inc(k_shifted, 1)

        def shift_v(t, first=False):
            if first:
                v_steps.start(t)
                v_steps.then_wait(pool.memset(v2[:, 0, :], 0.0))
            else:
                pool.wait_ge(pv_done, t)
                v_steps.start(t)
                v_steps.then_wait(copy(v2[:, 0, :], v2[:, 1, :]))
            pool.wait_ge(proj_taken, GROUPS * t + 3)
            copy(v2[:, 1, :], pv[:, V0:V0 + P]).then_inc(v_shifted, 1)

        def gate(t):
            pool.wait_ge(proj_taken, GROUPS * t + 4)
            pool.tensor_tensor(pv[:, C0:C0 + CONV_CH], pv[:, C0:C0 + CONV_CH], pv[:, H0:H0 + CONV_CH],
                               ALU.mult).then_inc(u_ready, 1)

        def history(t):
            pool.wait_ge(mix_parts, 3 * t - 2)
            copy(uT[:, :, 0:2], uT[:, :, P:P + 2]).then_inc(hist_ready, 1)

        def square_mix(t):
            pool.wait_ge(mix_parts, 3 * t + 3)
            s_steps.start(t)
            s_steps.then_wait(pool.tensor_tensor(squares, region2[:, D:2 * D], region2[:, D:2 * D], ALU.mult))
            s_steps.then_wait(pool.tensor_tensor(sqmix[:, 0:2, :], sqmix[:, 0:2, :], sqmix[:, 2:4, :], ALU.add))
            pool.tensor_tensor(sqmix[:, 0:8:4, :], sqmix[:, 0:8:4, :], sqmix[:, 1:8:4, :], ALU.add)
            pool.tensor_tensor(sqmix[:, 6, :], sqmix[:, 6, :], sqmix[:, 7, :], ALU.add).then_inc(mix_squared, 1)

        def tile(t, first=False, final=False):
            nxt = t + 1
            if not final:
                x_newton(nxt + 2)
            if not first:
                square_mix(t - 1)
            if final:
                return
            square_proj(nxt, wait_stats=not first)
            shift_k(nxt)
            q_norm(nxt + 2, pq[:, :])
            history(nxt)
            gate(nxt)
            shift_v(nxt)

        pool.memset(shared.three[:, :, :], 3.0)
        pool.memset(shared.eps4[:, :], 4 * EPS).then_inc(shared.consts_set, 1)
        pool.memset(uT[:, :, 0:2], 0.0).then_inc(hist_ready, 1)
        pool.memset(kT[:, 0:P], 0.0).then_inc(k_shifted, 1)
        pool.wait_ge(small_in, 32)
        pool.tensor_scalar(q8[:, 0:1], small[:, QG:QG + 1], HD ** -0.5, None, ALU.mult)
        pool.tensor_scalar(q8[:, 1:2], small[:, MQG:MQG + 1], HD ** -0.5, None, ALU.mult)
        pool.tensor_scalar(neg_sink[:, :], small[:, SINK:SINK + HEADS], -1.0, None, ALU.mult).then_inc(prepared, 1)
        for i in range(3):
            x_newton(i)
        for m in range(2):
            pool.wait_ge(kv_taken, m + 1)
            q_square(m, km_sq[:, :], km[m])
            q_norm(m, km[m], MEM_HEADS)
        pool.wait_ge(kv_done, 2)
        pool.memset(region[:, 0:HEADS * (KEYS + 1)], 0.0).then_inc(cleared, 1)
        pool.wait_ge(wl_ready, DC - 1)
        pool.tensor_copy(scores[:, :, KEYS], small[:, SINK:SINK + HEADS]).then_inc(sinks_set, 1)
        square_proj(0, wait_stats=False)
        q_norm(2, pq[:, :])
        gate(0)
        shift_v(0, first=True)
        tile(0, first=True)
        with pool.Fori(1, TILES - 2) as t:
            tile(t)
        tile(TILES - 2)
        tile(TILES - 1, final=True)
        low_mixed(pool, o, 0)
        pool.wait_ge(shared.consts_set, 1)
        group_newton(pool, o, shared)
        final_steps.square_mix = lambda: square_mix(TILES - 1)

    final_steps.free_banks = {(0, 0): (proj_taken, GROUPS * TILES), (1, 0): (proj_taken, GROUPS * TILES),
                              (0, 1): (exp_ready, UNITS * TILES), (1, 1): (exp_ready, UNITS * TILES),
                              (0, 2): (mix_parts, 3 * TILES - 1), (1, 2): (mix_parts, 3 * TILES)}
    final_steps.stats_free = (stats_taken, TILES)
    final_steps.slot1_free = (mix_parts, 3 * TILES - 1)
    final_steps.all_free = (mix_out, 16 * TILES)
    return final_steps


def out_resources(sem, half, d, mixed, tail, shared):
    o = Parts()
    o.half, o.first_tile = half, half * HT
    o.x, o.w_out, o.mixed, o.gains = d["x"], d["w_out"], mixed, shared.out_gains
    o.wh, o.wl = (a.rearrange("p (c n) -> p c n", c=DC) for a in (tail.high, tail.low))
    o.stage = [tail.raw[:, s * D:(s + 1) * D] for s in range(4)]
    o.mt, o.ys = tail.raw[:, 4 * D:5 * D], tail.raw[:, 5 * D:6 * D]
    o.mh, o.ml, o.y = tail.mh, tail.ml, tail.y
    o.stage_in = [sem(f"o{half}_stage{s}_in") for s in range(4)]
    o.mt_in = sem(f"o{half}_mt_in")
    o.y_in = [sem(f"o{half}_y{p}_in") for p in range(HT // 2)]
    o.wh_ready = sem(f"o{half}_wh_ready")
    o.wl_ready = sem(f"o{half}_wl_ready")
    o.mh_ready = sem(f"o{half}_mh_ready")
    o.ml_ready = sem(f"o{half}_ml_ready")
    return o


def out_phase(nc, block, sem, banks, half, tail, shared, o, before):
    wh, wl, mh, ml, y, ys, xh, xl = o.wh, o.wl, o.mh, o.ml, o.y, o.ys, tail.xh, tail.xl
    ident, gain, rall = shared.ident, shared.gain, shared.rall
    ssq, yv, yln, yr, yn2 = (shared.y_small[:, k:k + 1] for k in range(5))
    ml_ready = o.ml_ready
    turn = banks[0:2]
    parts = [banks[2:8:2], banks[3:8:2]]
    LAST = HT - 1

    out_done = sem(f"out_done_{half}")
    last_done = sem(f"last_done_{half}")
    last_taken = sem(f"last_taken_{half}")
    y_ready = sem(f"y_ready_{half}")
    yy_ready = sem(f"yy_ready_{half}")
    yr_ready = sem(f"yr_ready_{half}")
    ys_ready = sem(f"ys_ready_{half}")
    y_turned = sem(f"y_turned_{half}")
    yh_ready = sem(f"yh_ready_{half}")
    yl_ready = sem(f"yl_ready_{half}")
    act_y, pool_y, dve_y = sem(f"act_y_{half}"), sem(f"pool_y_{half}"), sem(f"dve_y_{half}")
    final_steps = Parts()
    final_steps.last_done, final_steps.last_taken, final_steps.w_out_split = last_done, last_taken, o.wl_ready
    final_steps.y_turned, final_steps.yl_ready = y_turned, yl_ready

    @block.sync
    def _(sp):
        with sp.Fori(3, HT) as j:
            sp.wait_ge(ml_ready, j)
            load_mixed(sp, o, j)
        if half == 0:
            sp.wait_ge(*before.all_free)

    @block.tensor
    def _(pe):
        def group(slot, n, g, first=False):
            if first:
                pe.wait_ge(*before.free_banks[n, g])
            return out_group(pe, o, parts, slot, n, g, split=0 if first and n == 0 else DC)

        def project(slot, n, first=False):
            for g in range(3):
                if first and half == 0 and g == 0:
                    continue
                done = group(slot, n, g, first)
            done.then_inc(out_done, 1)

        def turn_y(j, first=False):
            pe.wait_ge(ys_ready, j + 1)
            if first and half == 0:
                pe.wait_ge(*before.stats_free)
            for b in range(2):
                if not first:
                    pe.wait_ge(yl_ready, 2 * j + b - 1)
                for c in range(4):
                    done = pe.transpose(turn[b][:, c * P:(c + 1) * P], ys[:, (4 * b + c) * P:(4 * b + c + 1) * P],
                                        ident[:, :])
                done.then_inc(y_turned, 1)

        def tile(j, slot, first=False):
            pe.wait_ge(ml_ready, j + 1)
            for n in range(2):
                pe.wait_ge(y_ready, 2 * j + n - 1)
                project(slot, n)
                if first and half == 0 and n == 0:
                    before.mean_squares()
            turn_y(j - 1, first)

        pe.wait_ge(ml_ready, 1)
        project(0, 0, first=True)
        project(0, 1, first=True)
        tile(1, 1, first=True)
        with pe.Fori(1, HT // 2 - 1) as k:
            tile(2 * k, 0)
            tile(2 * k + 1, 1)
        tile(LAST - 1, 0)
        pe.wait_ge(ml_ready, LAST + 1)
        for g in range(3):
            pe.wait_ge(y_ready, 2 * LAST - 1)
            group(1, 0, g)
            pe.wait_ge(y_ready, 2 * LAST)
            group(1, 1, g).then_inc(last_done, 1)
        turn_y(LAST - 1)
        final_steps.turn_y = lambda: turn_y(LAST)

    @block.scalar
    def _(act):
        y_steps = Steps(act, act_y, 3)

        def y_rstd(j):
            if j == LAST:
                act.wait_ge(last_taken, 3)
            else:
                act.wait_ge(y_ready, 2 * j + 2)
            if j:
                act.wait_ge(y_turned, 2 * j)
            y_steps.start(j)
            y_steps.then_wait(act.activation(ys, y[:, j, :], ACT.Square, accum_out=ssq))
            y_steps.then_wait(act.activation(yv, ssq, ACT.Identity, bias=shared.eps4[:, :], scale=4.0 / D))
            rsqrt_table(act, y_steps, yr, yln, yv).then_inc(yy_ready, 1)

        def high_y(j):
            for b in range(2):
                act.wait_ge(y_turned, 2 * j + b + 1)
                act.activation(xh[:, 4 * b:4 * b + 4, j * P:(j + 1) * P],
                               turn[b][:, :].rearrange("p (c q) -> p c q", c=4), ACT.Copy).then_inc(yh_ready, 1)

        if half:
            act.preload_act_table_set(ACT_SET)
            group_table(act, o, shared)
        act.wait_ge(shared.consts_set, 1)
        act.wait_ge(*before.slot1_free)
        high_mixed(act, o, 1)
        for j in range(LAST):
            if j + 2 < HT:
                act.wait_ge(out_done, 2 * j + 2)
                high_mixed(act, o, j + 2)
            y_rstd(j)
            if j == 0:
                act.wait_ge(*before.all_free)
            if j < LAST - 1:
                high_y(j)
        final_steps.high_y, final_steps.y_rstd = high_y, y_rstd

    @block.vector
    def _(dve):
        y_steps = Steps(dve, dve_y, 4)

        def add(j, n, g):
            yn = y[:, j, n * BANK:(n + 1) * BANK]
            t = o.first_tile + j
            return dve.scalar_tensor_tensor(out=yn, in0=parts[n][g][:, :], scalar=rall[:, t, g:g + 1], in1=yn,
                                            op0=ALU.mult, op1=ALU.add)

        def add_groups(j):
            y_steps.start(j)
            for n in range(2):
                dve.wait_ge(out_done, 2 * j + n + 1)
                for g in range(2):
                    y_steps.then_wait(add(j, n, g))
                add(j, n, 2).then_inc(y_ready, 1)

        def add_last(g):
            dve.wait_ge(last_done, g + 1)
            add(LAST, 0, g)
            add(LAST, 1, g).then_inc(last_taken, 1)
            dve.wait_ge(last_taken, g + 1)

        def scale_y(j):
            dve.wait_ge(yr_ready, j + 1)
            dve.scalar_tensor_tensor(out=ys, in0=y[:, j, :], scalar=yr, in1=gain[:, :],
                                     op0=ALU.mult, op1=ALU.mult).then_inc(ys_ready, 1)

        def low_y(j):
            for b in range(2):
                dve.wait_ge(yh_ready, 2 * j + b + 1)
                part = slice(4 * b, 4 * b + 4)
                dve.tensor_tensor(xl[:, part, j * P:(j + 1) * P], turn[b][:, :].rearrange("p (c q) -> p c q", c=4),
                                  xh[:, part, j * P:(j + 1) * P], ALU.subtract).then_inc(yl_ready, 1)

        dve.wait_ge(shared.r_ready, half + 1)
        if half == 0:
            dve.wait_ge(shared.gain_ffn_in, 16)
        for j in range(LAST):
            if j % 2 == 0:
                dve.wait_ge(o.y_in[j // 2], 16)
            add_groups(j)
            scale_y(j)
            if half == 0 and j == 0:
                before.take_stats()
            if j:
                low_y(j - 1)
        final_steps.add, final_steps.scale_y, final_steps.low_y = add_last, scale_y, low_y

    @block.gpsimd
    def _(pool):
        y_steps = Steps(pool, pool_y, 3)

        def y_norm(j):
            pool.wait_ge(yy_ready, j + 1)
            y_steps.start(j)
            rsqrt_newton(pool, y_steps, yr, yv, yn2, shared.three[:, 0, 0:1]).then_inc(yr_ready, 1)

        if half:
            group_newton(pool, o, shared)
        pool.wait_ge(*before.slot1_free)
        low_mixed(pool, o, 1)
        if half == 0:
            before.square_mix()
        for j in range(HT):
            if j + 2 < HT:
                low_mixed(pool, o, j + 2)
            y_norm(j)

    return final_steps


def ffn_phase(nc, block, sem, banks, half, d, out, tail, shared, before, nxt):
    w_gu, w_down = d["w_gu"], d["w_down"]
    y, xh, xl = tail.y, tail.xh, tail.xl
    gu_raw = tail.raw[:, 0:4 * D].rearrange("p (c n) -> p c n", c=2)
    dn_raw = tail.raw[:, 4 * D:6 * D]
    gu_h, gu_l, hid_h, hid_l, dn_h, dn_l = (
        part for at in (slice(0, 4 * D), slice(4 * D, 6 * D), slice(6 * D, 8 * D)) for part in (tail.high[:, at], tail.low[:, at]))
    gu_h, gu_l, dn_h, dn_l = (a.rearrange("p (c n) -> p c n", c=2) for a in (gu_h, gu_l, dn_h, dn_l))
    hid_h, hid_l = (a.rearrange("p (t c n) -> p t c n", t=2, c=2) for a in (hid_h, hid_l))
    act_g, hid = tail.silu_gate, tail.hidden
    gate, up = banks[2:6:2], banks[3:6:2]
    down = [banks[6], banks[7], banks[0], banks[1]]
    DOWNS = HT

    gu_in = [sem(f"gu{c}_in_{half}") for c in range(2)]
    dn_in = sem(f"dn_in_{half}")
    guh_ready = sem(f"guh_ready_{half}")
    gul_ready = sem(f"gul_ready_{half}")
    dnh_ready = sem(f"dnh_ready_{half}")
    dnl_ready = sem(f"dnl_ready_{half}")
    gu_done = sem(f"gu_done_{half}")
    silu_ready = sem(f"silu_ready_{half}")
    hid_ready = sem(f"hid_ready_{half}")
    hh_ready = sem(f"hh_ready_{half}")
    hl_ready = sem(f"hl_ready_{half}")
    down_done = sem(f"down_done_{half}")
    y_added = sem(f"y_added_{half}")
    stored = sem(f"stored_{half}")
    first_tile = half * HT
    all_downs = 2 * DOWNS * PAIRS

    @block.sync
    def _(sp):
        def load_gu(c, q):
            sp.dma_start(gu_raw[:, c, :], w_gu[q]).then_inc(gu_in[c], 16)

        sp.wait_ge(before.w_out_split, DC)
        load_gu(0, 0)
        load_gu(1, 1)
        sp.wait_ge(before.y_turned, 2 * HT)
        sp.dma_start(dn_raw, w_down[0]).then_inc(dn_in, 16)
        with sp.Fori(1, PAIRS) as p:
            for c in range(2):
                sp.wait_ge(gul_ready, 2 * p + c - 1)
                load_gu(c, 2 * p + c)
            sp.wait_ge(dnl_ready, p)
            sp.dma_start(dn_raw, w_down[p]).then_inc(dn_in, 16)
        if nxt:
            for c in range(4):
                if c % 2 == 0:
                    sp.wait_ge(gul_ready, 2 * PAIRS - 1 + c // 2)
                load_w_out(sp, nxt, c)
            sp.wait_ge(dnl_ready, PAIRS)
            load_mixed(sp, nxt, 0)
            for c in range(4, 6):
                load_w_out(sp, nxt, c)
            sp.wait_ge(nxt.ml_ready, 1)
            load_mixed(sp, nxt, 1)
        for tb in range(2):
            for j in range(4):
                sp.wait_ge(y_added, all_downs - 2 * DOWNS + DOWNS * tb + 2 * j + 2)
                sp.dma_start(out[first_tile + 4 * tb + j], y[:, 4 * tb + j, :]).then_inc(stored, 16)
            if nxt:
                if tb == 0:
                    for c in range(6, DC):
                        load_w_out(sp, nxt, c)
                else:
                    sp.wait_ge(nxt.ml_ready, 2)
                    load_mixed(sp, nxt, 2)
                sp.wait_ge(stored, 16 * (4 * tb + 4))
                for part in range(2 * tb, 2 * tb + 2):
                    load_y(sp, nxt, part)
        sp.wait_ge(stored, 16 * HT)

    @block.tensor
    def _(pe):
        def unit(p, tb, c, wait_banks=True):
            n = 2 * tb + c
            pe.wait_ge(gul_ready, 2 * p + c + 1)
            if wait_banks:
                pe.wait_ge(hid_ready, 4 * p + n - 1)
            tokens = slice(tb * BANK, (tb + 1) * BANK)
            for k, to in enumerate((gate[c], up[c])):
                for dc in range(DC):
                    w = slice((k * DC + dc) * P, (k * DC + dc + 1) * P)
                    done = three_passes(pe, to[:, :], gu_h[:, c, w], gu_l[:, c, w], xh[:, dc, tokens], xl[:, dc, tokens],
                                        dc == 0, dc == DC - 1)
            done.then_inc(gu_done, 1)

        def down_block(p, tb, wait_banks=True):
            pe.wait_ge(dnl_ready, p + 1)
            pe.wait_ge(hl_ready, 4 * p + 2 * tb + 2)
            for g in range(DOWNS):
                j, n = g // 2, g % 2
                if wait_banks or g >= 4:
                    pe.wait_ge(y_added, 2 * DOWNS * p + DOWNS * tb + g - 3)
                cols = slice(n * BANK, (n + 1) * BANK)
                for c in range(2):
                    tok = slice(j * P, (j + 1) * P)
                    done = three_passes(pe, down[g % 4][:, :], hid_h[:, tb, c, tok], hid_l[:, tb, c, tok],
                                        dn_h[:, c, cols], dn_l[:, c, cols], c == 0, c == 1)
                done.then_inc(down_done, 1)

        def pair(p):
            unit(p, 0, 0)
            unit(p, 0, 1)
            down_block(p - 1, 1)
            unit(p, 1, 0)
            unit(p, 1, 1)
            down_block(p, 0)

        pe.wait_ge(before.yl_ready, HT)
        pe.wait_ge(before.last_taken, 1)
        unit(0, 0, 0, wait_banks=False)
        before.turn_y()
        pe.wait_ge(before.last_taken, 2)
        unit(0, 0, 1, wait_banks=False)
        pe.wait_ge(before.yl_ready, 2 * HT)
        unit(0, 1, 0)
        unit(0, 1, 1)
        pe.wait_ge(before.last_taken, 3)
        down_block(0, 0, wait_banks=False)
        with pe.Fori(1, PAIRS) as p:
            pair(p)
        down_block(PAIRS - 1, 1)

    @block.scalar
    def _(act):
        def high_gu(p, c, first=False):
            act.wait_ge(gu_in[c], 16 * p + 16)
            if not first:
                act.wait_ge(gu_done, 4 * p + c - 1)
            act.activation(gu_h[:, c, :], gu_raw[:, c, :], ACT.Copy).then_inc(guh_ready, 1)

        def high_down(p, first=False):
            act.wait_ge(dn_in, 16 * p + 16)
            if not first:
                act.wait_ge(down_done, 2 * DOWNS * p)
            act.activation(dn_h[:, :, :], dn_raw.rearrange("p (c n) -> p c n", c=2), ACT.Copy).then_inc(dnh_ready, 1)

        def hidden(p, tb, c, first=False):
            n = 2 * tb + c
            act.wait_ge(gu_done, 4 * p + n + 1)
            if not first:
                act.wait_ge(hid_ready, 4 * p + n)
            act.activation(act_g, gate[c][:, :], ACT.Silu).then_inc(silu_ready, 1)
            act.wait_ge(hid_ready, 4 * p + n + 1)
            act.activation(hid_h[:, tb, c, :], hid, ACT.Copy).then_inc(hh_ready, 1)

        def pair(p, first=False, final=False):
            hidden(p, 0, 0, first)
            hidden(p, 0, 1)
            if not first:
                high_down(p)
            hidden(p, 1, 0)
            if not final:
                high_gu(p + 1, 0)
            elif nxt:
                high_w_out(act, nxt, 0)
                high_w_out(act, nxt, 1)
            hidden(p, 1, 1)
            if not final:
                high_gu(p + 1, 1)
            elif nxt:
                high_w_out(act, nxt, 2)
                high_w_out(act, nxt, 3)
                high_mixed(act, nxt, 0)
                act.wait_ge(down_done, all_downs - DOWNS)
                high_w_out(act, nxt, 4)
                act.wait_ge(down_done, all_downs)
                for k in range(5, DC):
                    high_w_out(act, nxt, k)

        act.wait_ge(before.last_done, 1)
        high_gu(0, 0, first=True)
        before.high_y(HT - 2)
        before.y_rstd(HT - 1)
        high_gu(0, 1, first=True)
        before.high_y(HT - 1)
        high_down(0, first=True)
        pair(0, first=True)
        with act.Fori(1, PAIRS - 1) as p:
            pair(p)
        pair(PAIRS - 1, final=True)

    @block.vector
    def _(dve):
        def low_gu(p, c):
            dve.wait_ge(guh_ready, 2 * p + c + 1)
            dve.tensor_tensor(gu_l[:, c, :], gu_raw[:, c, :], gu_h[:, c, :], ALU.subtract).then_inc(gul_ready, 1)

        def low_down(p):
            dve.wait_ge(dnh_ready, p + 1)
            dve.tensor_tensor(dn_l[:, :, :], dn_raw.rearrange("p (c n) -> p c n", c=2), dn_h[:, :, :],
                              ALU.subtract).then_inc(dnl_ready, 1)

        def hidden(p, tb, c, first=False):
            n = 2 * tb + c
            dve.wait_ge(silu_ready, 4 * p + n + 1)
            if not first:
                dve.wait_ge(hl_ready, 4 * p + n)
            dve.tensor_tensor(hid, up[c][:, :], act_g, ALU.mult).then_inc(hid_ready, 1)
            dve.wait_ge(hh_ready, 4 * p + n + 1)
            dve.tensor_tensor(hid_l[:, tb, c, :], hid, hid_h[:, tb, c, :], ALU.subtract).then_inc(hl_ready, 1)

        def add_down(p, tb):
            for g in range(DOWNS):
                j, n = 4 * tb + g // 2, g % 2
                dve.wait_ge(down_done, 2 * DOWNS * p + DOWNS * tb + g + 1)
                yn = y[:, j, n * BANK:(n + 1) * BANK]
                dve.tensor_tensor(yn, down[g % 4][:, :], yn, ALU.add).then_inc(y_added, 1)

        def pair(p, first=False, final=False):
            hidden(p, 0, 0, first)
            hidden(p, 0, 1)
            if not first:
                add_down(p - 1, 1)
                low_down(p)
            hidden(p, 1, 0)
            if not final:
                low_gu(p + 1, 0)
            elif nxt:
                low_w_out(dve, nxt, 0)
                low_w_out(dve, nxt, 1)
            hidden(p, 1, 1)
            add_down(p, 0)
            if not final:
                low_gu(p + 1, 1)
            elif nxt:
                low_w_out(dve, nxt, 2)
                low_w_out(dve, nxt, 3)

        before.add(0)
        low_gu(0, 0)
        before.add(1)
        before.add(2)
        before.low_y(HT - 2)
        before.scale_y(HT - 1)
        low_gu(0, 1)
        before.low_y(HT - 1)
        low_down(0)
        pair(0, first=True)
        with dve.Fori(1, PAIRS - 1) as p:
            pair(p)
        pair(PAIRS - 1, final=True)
        if nxt:
            low_w_out(dve, nxt, 4)
        add_down(PAIRS - 1, 1)
        if nxt:
            for c in range(5, DC):
                low_w_out(dve, nxt, c)

    if nxt:
        @block.gpsimd
        def _(pool):
            low_mixed(pool, nxt, 0)

    banks_free = {(n, g): (hid_ready, 4 * PAIRS) for n in range(2) for g in range(2)}
    banks_free |= {(n, 2): (y_added, all_downs - 3 + n) for n in range(2)}
    final_steps = Parts()
    final_steps.free_banks, final_steps.slot1_free, final_steps.all_free = banks_free, (hl_ready, 4 * PAIRS), (gu_done, 4 * PAIRS)
    return final_steps


def tail_memory(nc):
    with ExitStack() as place:
        def sb(name, shape, dt=F32):
            return place.enter_context(nc.sbuf_tensor(name, shape, dt))

        t = Parts()
        t.high = sb("weights_high", [P, DC * D], F32R)[:, :]
        t.low = sb("weights_low", [P, DC * D], F32R)[:, :]
        t.raw = sb("weights_raw", [P, 6 * D])[:, :]
        t.y = sb("y", [P, HT, D])
        mh0, ml0, mh1 = (sb(name, [P, DC, P], F32R) for name in ("mixed_high0", "mixed_low0", "mixed_high1"))
        with nc.sbuf_tensor("silu_and_hidden", [P, 2, BANK], F32) as silu_and_hidden:
            t.silu_gate, t.hidden = silu_and_hidden[:, 0, :], silu_and_hidden[:, 1, :]
        ml1 = sb("mixed_low1", [P, DC, P], F32R)
        t.mh, t.ml = [mh0, mh1], [ml0, ml1]
        t.xh = sb("y_high", [P, DC, HALF], F32R)
        t.xl = sb("y_low", [P, DC, HALF], F32R)
    return t


def layer(nc, d, out):
    mixed = nc.dram_tensor("mixed", (TILES, P, D), F32, kind="Internal").ap()
    with ExitStack() as ctx:
        def sb(name, shape):
            return ctx.enter_context(nc.sbuf_tensor(name, shape, F32))

        def sem(name):
            return ctx.enter_context(nc.semaphore(name))

        shared = Parts()
        shared.gain = sb("gain_row", [P, D])
        shared.ident = sb("ident", [P, P])
        shared.stats = sb("group_stats", [P, TILES, 3])
        shared.rall = sb("group_rstds", [P, TILES, 3])
        shared.tmp = sb("group_tmp", [P, TILES, 3])
        shared.three = sb("three", [P, TILES, 3])
        shared.eps4 = sb("eps4", [P, 1])
        shared.y_small = sb("y_small", [P, 5])
        shared.out_gains = sb("out_gains", [P, DC])
        shared.consts_set = sem("consts_set")
        shared.out_gains_in = sem("out_gains_in")
        shared.gain_ffn_in = sem("gain_ffn_in")
        shared.r_ln, shared.r_table = sem("r_ln"), sem("r_table")
        shared.r_pool, shared.r_ready = sem("r_pool"), sem("r_ready")
        banks = [ctx.enter_context(nc.psum_tensor(f"bank{k}", [P, BANK], F32)) for k in range(8)]
        tail = tail_memory(nc)
        outs = [out_resources(sem, half, d, mixed, tail, shared) for half in range(2)]
        with nc.Block() as block:
            before = mixer_phase(nc, block, sem, banks, d, mixed, shared, outs[0])
            for half in range(2):
                before = out_phase(nc, block, sem, banks, half, tail, shared, outs[half], before)
                before = ffn_phase(nc, block, sem, banks, half, d, out, tail, shared, before, outs[1] if half == 0 else None)

def lay_out(i):
    def rows(a, *shape):
        return np.ascontiguousarray(a, dtype=a.dtype).reshape(shape)

    def by_partition(w):
        return np.ascontiguousarray(w.reshape(-1, P, w.shape[-1]).transpose(1, 0, 2))

    w_in = i["w_in"][0]
    heads = [h for j in range(4) for h in (j, 4 + j)]
    q = w_in[:, :512].reshape(D, HEADS, HD)[:, heads].reshape(D, 512)
    k, v = w_in[:, 512:640], w_in[:, 640:768]
    h, b, c, mq = (w_in[:, 768 + 256 * n:1024 + 256 * n] for n in range(4))
    cols = np.zeros((P, COLS), np.float32)
    for at, name in ((QG, "q_norm"), (KG, "k_norm"), (MQG, "mem_q_norm"), (MKG, "mem_k_norm")):
        cols[:, at] = np.concatenate([i[name][0]] * 2)
    for ch in range(CC):
        cols[:, CW + 3 * ch:CW + 3 * ch + 3] = i["conv_w"][0][:, ch * P:(ch + 1) * P].T
        cols[:, CB + ch] = i["conv_b"][0][ch * P:(ch + 1) * P]
    cols[:, SINK:SINK + HEADS] = i["attn_sinks"][0][None, :]
    cols[:, MEANS:MEANS + 3] = [4 / 512, 4 / 256, 4 / 256]
    cols[:, EPS4] = 4 * EPS
    cols[:, THREE] = 3.0
    cols[:, ONE] = 1.0
    cols[:, GAIN:GAIN + DC] = i["norm_mix"][0].reshape(DC, P).T
    dist = (np.arange(P)[:, None] + P - np.arange(KEYS)[None, :])
    slopes = (2.0 ** (-8.0 * np.arange(1, HEADS + 1) / HEADS)).astype(np.float32)
    bias = -slopes[None, :, None] * dist[:, None, :].astype(np.float32)
    masks = np.where(((dist >= 0) & (dist < P))[:, None, :], bias, np.float32(MASKED)).astype(np.float32)
    order = np.concatenate([np.arange(h * HD, h * HD + HD) for h in heads] + [np.arange(512, 1024)])
    w_out = i["w_out"][0][order]
    out_gain = np.concatenate([i["out_norm_attn"][0], i["out_norm_conv"][0], i["out_norm_mem"][0]])[order]
    gate, up = (i[n][0].reshape(DC, P, 2 * PAIRS, P) for n in ("w_gate", "w_up"))
    w_gu = np.stack([gate, up]).transpose(3, 2, 0, 1, 4)
    w_down = i["w_down"][0].reshape(PAIRS, 2, P, D).transpose(0, 2, 1, 3)
    return {
        "x": rows(i["x"], TILES, P, D),
        "x_turned": np.ascontiguousarray(i["x"].reshape(TILES, P, DC, P).transpose(0, 3, 2, 1)).reshape(TILES, P, D),
        "mem": rows(i["mem"], 2, P, D),
        "cols": cols,
        "gain_mem": np.repeat(i["norm_mem"], P, axis=0),
        "gain_ffn": np.repeat(i["norm_ffn"], P, axis=0),
        "masks": masks,
        "ident": np.eye(P, dtype=np.float32),
        "w_in": by_partition(np.concatenate([q, k, mq, v, h, c, b], axis=1)),
        "w_mem": by_partition(i["w_mem_kv"][0]).reshape(P, -1),
        "w_out": by_partition(w_out),
        "out_gain": np.ascontiguousarray(out_gain.reshape(DC, P).T),
        "w_gu": np.ascontiguousarray(w_gu).reshape(2 * PAIRS, P, 2 * DC * P),
        "w_down": np.ascontiguousarray(w_down).reshape(PAIRS, P, 2 * D),
    }


def kernel(**inputs):
    from concourse import bacc
    from concourse.bass_utils import run_bass_kernel_spmd

    nc = bacc.Bacc("TRN2", target_bir_lowering=False, num_devices=1)
    arrays = {f"in_{n}": a for n, a in lay_out({n: np.asarray(a) for n, a in inputs.items()}).items()}
    aps = {n[3:]: nc.dram_tensor(n, a.shape, F32, kind="ExternalInput").ap() for n, a in arrays.items()}
    out = nc.dram_tensor("out", (TILES, P, D), F32, kind="ExternalOutput").ap()
    layer(nc, aps, out)
    return run_bass_kernel_spmd(nc, [arrays], core_ids=[0]).results[0]["out"].reshape(1, SEQ, D)
```
